# Optimizing a Trainium2 kernel written in Bass

```python
import math
import jax, jax.numpy as jnp
from jax import lax
import numpy as np

D_MODEL = 1024
BATCH = 1
SEQ = 2048
DEPTH = 1
DEC_BATCH = 8
DEC_SEQ = 8
PAST_LEN = 8192
PAGE_SIZE = 128

MIX_WIDTH = D_MODEL
ATT_WIDTH = MIX_WIDTH // 2
HEAD_DIM = 64
N_HEADS = ATT_WIDTH // HEAD_DIM
POOL_WIDTH = MIX_WIDTH - ATT_WIDTH
POOL_WINDOWS = (2, 4, 8, 16)
N_POOL_GROUPS = len(POOL_WINDOWS)
POOL_GROUP_DIM = POOL_WIDTH // N_POOL_GROUPS
MAX_WINDOW = max(POOL_WINDOWS)
IN_WIDTH = 3 * ATT_WIDTH + N_HEADS + POOL_WIDTH
D_FF = ((8 * D_MODEL // 3 + 127) // 128) * 128
CONV_WIDTH = 3
Q_BLOCK = 128
LN_EPS = 1e-5
ATTN_SCALE = HEAD_DIM ** -0.5
ALPHA = (2 * DEPTH) ** 0.25
BETA = (8 * DEPTH) ** -0.25
FORGET_BIAS_MIN = 3.0
FORGET_BIAS_MAX = 10.0
FORGET_W_SCALE = 0.1
NEG_INF = -1e30

kernel_name = "hymba_fox_pool_convffn_step"

def _layer_norm(x, g, b):
    xf = x.astype(jnp.float32)
    mu = jnp.mean(xf, axis=-1, keepdims=True)
    var = jnp.mean(jnp.square(xf - mu), axis=-1, keepdims=True)
    y = (xf - mu) * lax.rsqrt(var + LN_EPS) * g.astype(jnp.float32) + b.astype(jnp.float32)
    return y.astype(x.dtype)

def _mixer_proj(x, w_in, b_f):
    B, T = x.shape[0], x.shape[1]
    p = jnp.einsum('btd,de->bte', x, w_in)
    q = p[..., :ATT_WIDTH].reshape(B, T, N_HEADS, HEAD_DIM)
    k = p[..., ATT_WIDTH:2 * ATT_WIDTH].reshape(B, T, N_HEADS, HEAD_DIM)
    v = p[..., 2 * ATT_WIDTH:3 * ATT_WIDTH].reshape(B, T, N_HEADS, HEAD_DIM)
    f_logit = p[..., 3 * ATT_WIDTH:3 * ATT_WIDTH + N_HEADS]
    u = p[..., 3 * ATT_WIDTH + N_HEADS:]
    logf = jax.nn.log_sigmoid(f_logit.astype(jnp.float32) + b_f.astype(jnp.float32))
    return q, k, v, logf, u

def _attend_block(q, k, v, qc, kc, q_pos, k_pos):
    s = jnp.einsum('bqhd,bkhd->bhqk', q, k).astype(jnp.float32) * ATTN_SCALE
    s = s + jnp.swapaxes(qc, 1, 2)[..., :, None] - jnp.swapaxes(kc, 1, 2)[..., None, :]
    causal = (q_pos[:, None] >= k_pos[None, :])[None, None]
    s = jnp.where(causal, s, NEG_INF)
    p = jax.nn.softmax(s, axis=-1)
    return jnp.einsum('bhqk,bkhd->bqhd', p.astype(v.dtype), v)

def _forget_attention(q, k, v, qc, kc, q_pos, k_pos, n_past):
    T = q.shape[1]
    outs = []
    for start in range(0, T, Q_BLOCK):
        end = min(start + Q_BLOCK, T)
        kend = n_past + end
        outs.append(_attend_block(q[:, start:end], k[:, :kend], v[:, :kend],
                                  qc[:, start:end], kc[:, :kend],
                                  q_pos[start:end], k_pos[:kend]))
    return jnp.concatenate(outs, axis=1)

def _multi_pool(u, buf, pos, w_pool, pool_scale):
    B, T = u.shape[0], u.shape[1]
    full = jnp.concatenate([buf.astype(u.dtype), u], axis=1)
    cs = jnp.cumsum(full.astype(jnp.float32), axis=1)
    cs = jnp.concatenate([jnp.zeros((B, 1, POOL_WIDTH), jnp.float32), cs], axis=1)
    uf = u.astype(jnp.float32)
    groups = []
    for g, w in enumerate(POOL_WINDOWS):
        lo, hi = g * POOL_GROUP_DIM, (g + 1) * POOL_GROUP_DIM
        end = cs[:, MAX_WINDOW:MAX_WINDOW + T, lo:hi]
        start = cs[:, MAX_WINDOW - w:MAX_WINDOW - w + T, lo:hi]
        cnt = jnp.minimum(pos + 1, w).astype(jnp.float32)[None, :, None]
        groups.append((end - start) / cnt - uf[..., lo:hi])
    pooled = jnp.stack(groups, axis=2).astype(u.dtype)
    mixed = jnp.einsum('btgc,gce->btge', pooled, w_pool).reshape(B, T, POOL_WIDTH)
    return mixed * pool_scale, full[:, T:]

def _conv_ffn(x, buf, w_up, b_up, w_conv, b_conv, w_down):
    T = x.shape[1]
    h = jnp.einsum('btd,df->btf', x, w_up) + b_up
    full = jnp.concatenate([buf.astype(h.dtype), h], axis=1)
    hc = b_conv + full[:, 0:T] * w_conv[0]
    for j in range(1, CONV_WIDTH):
        hc = hc + full[:, j:j + T] * w_conv[j]
    gate, val = hc[..., :D_FF], hc[..., D_FF:]
    out = jnp.einsum('btf,fd->btd', jax.nn.gelu(gate) * val, w_down)
    return out, full[:, T:]

def _layer(x, pos, k_past, v_past, kc_past, pool_buf, conv_buf,
           w_in, b_f, w_pool, pool_scale, w_out, ln1_g, ln1_b,
           w_up, b_up, w_conv, b_conv, w_down, ln2_g, ln2_b):
    B, T = x.shape[0], x.shape[1]
    n_past = k_past.shape[1]
    q, k, v, logf, u = _mixer_proj(x, w_in, b_f)
    qc = jnp.cumsum(logf, axis=1)
    kc = jnp.concatenate([kc_past, qc], axis=1)
    k_all = jnp.concatenate([k_past.astype(k.dtype), k], axis=1)
    v_all = jnp.concatenate([v_past.astype(v.dtype), v], axis=1)
    k_pos = jnp.arange(n_past + T, dtype=jnp.int32) + (pos[0] - n_past)
    att = _forget_attention(q, k_all, v_all, qc, kc, pos, k_pos, n_past)
    att = att.reshape(B, T, ATT_WIDTH)
    pool, new_pool = _multi_pool(u, pool_buf, pos, w_pool, pool_scale)
    mix = jnp.einsum('bte,ed->btd', jnp.concatenate([att, pool], axis=-1), w_out)
    x1 = _layer_norm(ALPHA * x + mix, ln1_g, ln1_b)
    ff, new_conv = _conv_ffn(x1, conv_buf, w_up, b_up, w_conv, b_conv, w_down)
    x2 = _layer_norm(ALPHA * x1 + ff, ln2_g, ln2_b)
    return x2, k, v, logf, new_pool, new_conv

def setup_inputs(seed: int = 0) -> dict:
    key = jax.random.key(seed)
    ks = jax.random.split(key, 24)
    f32 = jnp.float32
    n_pages = PAST_LEN // PAGE_SIZE
    n_used = DEC_BATCH * n_pages
    n_pool_pages = (n_used * 5) // 4
    nrm = lambda k, s: jax.random.normal(k, s, f32)
    x_prompt = nrm(ks[0], (BATCH, SEQ, D_MODEL))
    x_sample = nrm(ks[1], (DEC_BATCH, DEC_SEQ, D_MODEL))
    b_f = jnp.linspace(FORGET_BIAS_MIN, FORGET_BIAS_MAX, N_HEADS, dtype=f32)[None, :] \
        + 0.1 * nrm(ks[9], (DEPTH, N_HEADS))
    cache_k = nrm(ks[2], (DEPTH, n_pool_pages, PAGE_SIZE, N_HEADS, HEAD_DIM))
    cache_v = nrm(ks[3], (DEPTH, n_pool_pages, PAGE_SIZE, N_HEADS, HEAD_DIM))
    cache_logf = jax.nn.log_sigmoid(b_f[:, None, None, :]
                                    + 0.3 * nrm(ks[4], (DEPTH, n_pool_pages, PAGE_SIZE, N_HEADS)))
    state_pool = nrm(ks[5], (DEPTH, DEC_BATCH, MAX_WINDOW - 1, POOL_WIDTH))
    state_conv = nrm(ks[6], (DEPTH, DEC_BATCH, CONV_WIDTH - 1, 2 * D_FF))
    page_table = jax.random.permutation(ks[7], n_pool_pages)[:n_used].reshape(DEC_BATCH, n_pages).astype(jnp.int32)
    w_in = nrm(ks[8], (DEPTH, D_MODEL, IN_WIDTH)) * D_MODEL ** -0.5
    w_in = w_in.at[:, :, 3 * ATT_WIDTH:3 * ATT_WIDTH + N_HEADS].multiply(FORGET_W_SCALE)
    w_pool = nrm(ks[10], (DEPTH, N_POOL_GROUPS, POOL_GROUP_DIM, POOL_GROUP_DIM)) * POOL_GROUP_DIM ** -0.5
    pool_scale = 1.0 + 0.1 * nrm(ks[11], (DEPTH, POOL_WIDTH))
    w_out = nrm(ks[12], (DEPTH, MIX_WIDTH, D_MODEL)) * (MIX_WIDTH ** -0.5) * BETA
    ln1_g = 1.0 + 0.05 * nrm(ks[13], (DEPTH, D_MODEL))
    ln1_b = 0.02 * nrm(ks[14], (DEPTH, D_MODEL))
    w_up = nrm(ks[15], (DEPTH, D_MODEL, 2 * D_FF)) * D_MODEL ** -0.5
    b_up = 0.02 * nrm(ks[16], (DEPTH, 2 * D_FF))
    w_conv = nrm(ks[17], (DEPTH, CONV_WIDTH, 2 * D_FF)) * CONV_WIDTH ** -0.5
    b_conv = 0.02 * nrm(ks[18], (DEPTH, 2 * D_FF))
    w_down = nrm(ks[19], (DEPTH, D_FF, D_MODEL)) * (D_FF ** -0.5) * BETA
    ln2_g = 1.0 + 0.05 * nrm(ks[20], (DEPTH, D_MODEL))
    ln2_b = 0.02 * nrm(ks[21], (DEPTH, D_MODEL))
    return {"x_prompt": x_prompt, "x_sample": x_sample,
            "cache_k": cache_k, "cache_v": cache_v, "cache_logf": cache_logf,
            "state_pool": state_pool, "state_conv": state_conv, "page_table": page_table,
            "w_in": w_in, "b_f": b_f, "w_pool": w_pool, "pool_scale": pool_scale,
            "w_out": w_out, "ln1_g": ln1_g, "ln1_b": ln1_b,
            "w_up": w_up, "b_up": b_up, "w_conv": w_conv, "b_conv": b_conv,
            "w_down": w_down, "ln2_g": ln2_g, "ln2_b": ln2_b}

def reference(x_prompt, x_sample, cache_k, cache_v, cache_logf, state_pool, state_conv,
              page_table, w_in, b_f, w_pool, pool_scale, w_out, ln1_g, ln1_b,
              w_up, b_up, w_conv, b_conv, w_down, ln2_g, ln2_b):
    B, T_p = x_prompt.shape[0], x_prompt.shape[1]
    DB, T_s = x_sample.shape[0], x_sample.shape[1]
    n_pages = page_table.shape[1]
    n_past = n_pages * PAGE_SIZE
    pos_p = jnp.arange(T_p, dtype=jnp.int32)
    pos_s = n_past + jnp.arange(T_s, dtype=jnp.int32)
    empty_kv = jnp.zeros((B, 0, N_HEADS, HEAD_DIM), x_prompt.dtype)
    empty_kc = jnp.zeros((B, 0, N_HEADS), jnp.float32)
    zero_pool = jnp.zeros((B, MAX_WINDOW - 1, POOL_WIDTH), x_prompt.dtype)
    zero_conv = jnp.zeros((B, CONV_WIDTH - 1, 2 * D_FF), x_prompt.dtype)
    yp, ys = x_prompt, x_sample
    kp_l, vp_l, fp_l, pp_l, cp_l = [], [], [], [], []
    ks_l, vs_l, fs_l, ps_l, cs_l = [], [], [], [], []
    for l in range(DEPTH):
        weights = (w_in[l], b_f[l], w_pool[l], pool_scale[l], w_out[l], ln1_g[l], ln1_b[l],
                   w_up[l], b_up[l], w_conv[l], b_conv[l], w_down[l], ln2_g[l], ln2_b[l])
        yp, kp, vp, fp, pp, cp = _layer(yp, pos_p, empty_kv, empty_kv, empty_kc,
                                        zero_pool, zero_conv, *weights)
        k_past = cache_k[l][page_table].reshape(DB, n_past, N_HEADS, HEAD_DIM)
        v_past = cache_v[l][page_table].reshape(DB, n_past, N_HEADS, HEAD_DIM)
        lf_past = cache_logf[l][page_table].reshape(DB, n_past, N_HEADS).astype(jnp.float32)
        kc_past = lf_past - lax.cumsum(lf_past, axis=1, reverse=True)
        ys, ksn, vsn, fsn, psn, csn = _layer(ys, pos_s, k_past, v_past, kc_past,
                                             state_pool[l], state_conv[l], *weights)
        kp_l.append(kp); vp_l.append(vp); fp_l.append(fp); pp_l.append(pp); cp_l.append(cp)
        ks_l.append(ksn); vs_l.append(vsn); fs_l.append(fsn); ps_l.append(psn); cs_l.append(csn)
    return (yp, ys,
            jnp.stack(kp_l, 0), jnp.stack(vp_l, 0), jnp.stack(fp_l, 0),
            jnp.stack(pp_l, 0), jnp.stack(cp_l, 0),
            jnp.stack(ks_l, 0), jnp.stack(vs_l, 0), jnp.stack(fs_l, 0),
            jnp.stack(ps_l, 0), jnp.stack(cs_l, 0))


_drawn_inputs = setup_inputs


def setup_inputs(seed=0):
    import zlib

    import numpy as np

    out = dict(_drawn_inputs(seed))
    spreads = {}
    factors = {'ln1_b': 2.726, 'b_up': 2.821, 'b_conv': 6.399, 'ln2_b': 2.754}
    for name, (base, spread) in spreads.items():
        noise = np.random.default_rng([zlib.crc32(name.encode()), seed]).standard_normal(out[name].shape)
        drawn = base * np.exp(spread * noise) if base else spread * noise
        out[name] = __import__('jax').numpy.asarray(drawn.astype(out[name].dtype))
    for name, factor in factors.items():
        out[name] = (out[name] * factor).astype(out[name].dtype)
    return out
```

```python
from contextlib import ExitStack

import numpy as np

import concourse.bass as bass
from concourse import mybir

F32 = mybir.dt.float32
BF16 = mybir.dt.bfloat16
I32 = mybir.dt.int32
ALU = mybir.AluOpType
ACT = mybir.ActivationFunctionType
AXX = mybir.AxisListType.X

P = 128
D = 1024
DC = D // P
SEQ = 2048
NB, NT = 8, 8
S = NB * NT
H, HD = 8, 64
AW = H * HD
AC = AW // P
PW = 512
G = 4
MAXW = 16
IW = 3 * AW + H + PW
UO = 3 * AW + H
FF = 2816
FC = FF // P
PAGE = 128
NPG = 64
NPOOL = 640
TILES = SEQ // P
SCALE = HD ** -0.5
ALPHA = 2.0 ** 0.25
EPS = 1e-5
NEG = -1e30
TB = 512
BLOCKS = SEQ // TB
ds = bass.ds


class Mem:

    def __init__(self, nc, ctx, tag):
        self.nc, self.ctx, self.tag, self.sems = nc, ctx, tag, []
        ctx.callback(self.clear)

    def sb(self, name, shape, dt=F32):
        return self.ctx.enter_context(self.nc.sbuf_tensor(f"{self.tag}_{name}", shape, dt))

    def ps(self, name, shape, dt=F32):
        return self.ctx.enter_context(self.nc.psum_tensor(f"{self.tag}_ps_{name}", shape, dt))

    def sem(self, name):
        self.sems.append(self.nc.alloc_semaphore(name=f"{self.tag}_{name}"))
        return self.sems[-1]

    def clear(self):
        if self.sems:
            self.nc.clear_and_free_semaphores(self.sems)
            self.nc.all_engine_barrier()


class Link:

    def __init__(self, eng, sem):
        self.eng, self.sem, self.base, self.n = eng, sem, 0, 0

    def __call__(self, ins):
        self.n += 1
        ins.then_inc(self.sem, 1)
        self.eng.wait_ge(self.sem, self.base + self.n)

    def enter(self, base):
        self.base, self.n = base, 0


def stage_project(nc, io, sc, persist):
    NG = 5
    GC = [412, 412, 412, 412, 408]
    GO = [sum(GC[:g]) for g in range(NG)]
    assert sum(GC) == IW
    with ExitStack() as ctx:
        m = Mem(nc, ctx, "A")
        ident, uT, fgate, psamp, uTs = persist["ident"], persist["uT"], persist["fgate"], persist["psamp"], persist["uTs"]
        w = m.sb("w", [P, DC, IW])
        xin = m.sb("xin", [P, 2, D])
        xT = m.sb("xT", [P, 2, DC, P])
        prow = m.sb("prow", [P, 2, IW])
        qkT = m.sb("qkT", [P, 2, 2 * AC, P])
        stp = m.sb("stp", [P, PW])
        ps_x = m.ps("x", [P, 2, 512])
        ps_p = m.ps("p", [P, 2, 512])
        ps_t = m.ps("t", [P, 3, 512])

        w_in = m.sem("w_in")
        x_in = [m.sem("x_in0"), m.sem("x_in1")]
        st_in = m.sem("st_in")
        x_read = m.sem("x_read")
        xT_act, xT_dve = m.sem("xT_act"), m.sem("xT_dve")
        proj = [m.sem("proj0"), m.sem("proj1")]
        prow_act, prow_dve = m.sem("prow_act"), m.sem("prow_dve")
        tr = m.sem("tr")
        trq, trk, tru = m.sem("trq"), m.sem("trk"), m.sem("tru")
        stored = [m.sem("stored0"), m.sem("stored1")]
        tail = m.sem("tail")
        tail_copied = m.sem("tail_copied")
        st_done = m.sem("st_done")
        gate_kept = m.sem("gate_kept")

        block = ctx.enter_context(nc.Block())

        @block.sync
        def _(sp):
            sp.dma_start(ident[:, :], io["c_ident"]).then_inc(w_in, 16)
            sp.dma_start(xin[:, 0, :], io["x_prompt"][0, 0:P, :]).then_inc(x_in[0], 16)
            for c in range(DC):
                sp.dma_start(w[:, c, :], io["w_in"][0, c * P:(c + 1) * P, :]).then_inc(w_in, 16)
            sp.dma_start(stp[0:NB * (MAXW - 1), :],
                         io["state_pool"].rearrange("a b w c -> (a b w) c")).then_inc(st_in, 16)

            def load(t, buf):
                sp.wait_ge(x_read, t - 1)
                sp.dma_start(xin[:, buf, :], io["x_prompt"][0, ds(t * P, P), :]).then_inc(x_in[buf], 16)

            sp.dma_start(xin[:, 1, :], io["x_prompt"][0, P:2 * P, :]).then_inc(x_in[1], 16)
            with sp.Fori(0, TILES // 2 - 1) as i:
                for par in range(2):
                    load(2 * i + par + 2, par)
            sp.wait_ge(x_read, TILES - 1)
            sp.dma_start(xin[0:S, 0, :], io["x_sample"].rearrange("b t d -> (b t) d")).then_inc(x_in[0], 16)
            sp.wait_ge(prow_act, NG * 8)
            sp.wait_ge(prow_dve, NG * 8)
            sp.dma_start(io["pool_prompt"], prow[P - (MAXW - 1):P, 1, UO:IW]).then_inc(st_done, 16)
            sp.wait_ge(prow_act, NG * 8 + 3)
            sp.wait_ge(prow_dve, NG * 8 + 2)
            sp.dma_start(io["k_sample"], psamp[0:S, AW:2 * AW]).then_inc(st_done, 16)
            sp.dma_start(io["v_sample"], psamp[0:S, 2 * AW:3 * AW]).then_inc(st_done, 16)
            sp.dma_start(sc["q_s"], psamp[0:S, 0:AW]).then_inc(st_done, 16)
            sp.dma_start(io["pool_sample"][:, 0:MAXW - 1 - NT, :],
                         io["state_pool"][0, :, NT:MAXW - 1, :]).then_inc(st_done, 16)
            for b in range(NB):
                sp.dma_start(io["pool_sample"][b, MAXW - 1 - NT:MAXW - 1, :],
                             psamp[b * NT:(b + 1) * NT, UO:IW]).then_inc(st_done, 16)
            sp.wait_ge(st_done, 16 * (5 + NB))
            for par in range(2):
                sp.wait_ge(stored[par], 48 * (TILES // 2))

        @block.tensor
        def _(pe):
            def x_transposes(t, count, par):
                pe.wait_ge(x_in[par], 16 * count)
                pe.wait_ge(xT_act, t)
                pe.wait_ge(xT_dve, t)
                for c in range(DC):
                    last = nc.tensor.transpose(ps_x[:, c // 4, (c % 4) * P:(c % 4 + 1) * P],
                                               xin[:, par, c * P:(c + 1) * P], ident[:, :])
                last.then_inc(x_read, 1)

            def project(t, i, par):
                pe.wait_ge(xT_act, t + 1)
                pe.wait_ge(xT_dve, t + 1)
                for g in range(NG):
                    n = NG * par + g
                    bank, use = n % 2, NG * i + n // 2
                    pe.wait_ge(prow_dve if bank else prow_act, use)
                    for c in range(DC):
                        last = nc.tensor.matmul(ps_p[:, bank, 0:GC[g]], xT[:, par, c, :],
                                                w[:, c, GO[g]:GO[g] + GC[g]], start=c == 0, stop=c == DC - 1)
                    last.then_inc(proj[bank], 1)

            def qku_transposes(t, i, par):
                pe.wait_ge(prow_act, NG * i + (3 if par == 0 else 5))
                pe.wait_ge(prow_dve, NG * i + (2 if par == 0 else 5))
                pe.wait_ge(trq, t)
                pe.wait_ge(trk, t)
                pe.wait_ge(tru, t)
                for j, off in enumerate((0, AW, UO)):
                    for c in range(4):
                        last = nc.tensor.transpose(ps_t[:, j, c * P:(c + 1) * P],
                                                   prow[:, par, off + c * P:off + (c + 1) * P], ident[:, :])
                last.then_inc(tr, 1)

            pe.wait_ge(w_in, 16 * (1 + DC))
            x_transposes(0, 1, 0)
            with pe.Fori(0, TILES // 2) as i:
                for par in range(2):
                    t = 2 * i + par
                    project(t, i, par)
                    x_transposes(t + 1, i + 1 + par, 1 - par)
                    qku_transposes(t, i, par)
            project(TILES, TILES // 2, 0)
            pe.wait_ge(prow_act, NG * 8 + 3)
            pe.wait_ge(prow_dve, NG * 8 + 2)
            pe.wait_ge(st_in, 16)
            pe.wait_ge(trk, TILES)
            pe.wait_ge(tru, TILES)
            for c in range(4):
                nc.tensor.transpose(ps_t[:, 1, c * S:(c + 1) * S], psamp[0:S, UO + c * P:UO + (c + 1) * P],
                                    ident[0:S, 0:S])
            n = NB * (MAXW - 1)
            for c in range(4):
                last = nc.tensor.transpose(ps_t[:, 2, c * P:c * P + n], stp[0:n, c * P:(c + 1) * P],
                                           ident[0:n, 0:n])
            last.then_inc(tail, 1)

        @block.scalar
        def _(act):
            def x_out(t, par):
                act.wait_ge(x_read, t + 1)
                nc.scalar.copy(xT[:, par, 0:4, :], ps_x[:, 0, :].rearrange("p (c t) -> p c t", c=4)).then_inc(xT_act, 1)

            def groups(i, par, dst):
                for g in range(NG):
                    n = NG * par + g
                    if n % 2 == 0:
                        act.wait_ge(proj[0], NG * i + n // 2 + 1)
                        nc.scalar.copy(dst[:, GO[g]:GO[g] + GC[g]], ps_p[:, 0, 0:GC[g]]).then_inc(prow_act, 1)

            def store(t, i, par):
                row = prow[:, par, :]
                act.wait_ge(prow_act, NG * i + (3 if par == 0 else 5))
                act.wait_ge(prow_dve, NG * i + (2 if par == 0 else 5))
                act.dma_start(io["k_prompt"][ds(t * P, P), :], row[:, AW:2 * AW]).then_inc(stored[par], 16)
                act.dma_start(io["v_prompt"][ds(t * P, P), :], row[:, 2 * AW:3 * AW]).then_inc(stored[par], 16)
                act.wait_ge(trq, t + 1)
                act.wait_ge(trk, t + 1)
                act.dma_start(sc["qkT"][:, :, ds(t * P, P)].rearrange("a p t -> p a t"),
                              qkT[:, par, :, :]).then_inc(stored[par], 16)

            x_out(0, 0)
            with act.Fori(0, TILES // 2) as i:
                for par in range(2):
                    t = 2 * i + par
                    act.wait_ge(stored[par], 48 * i)
                    act.wait_ge(gate_kept, 2 * i)
                    groups(i, par, prow[:, par, :])
                    x_out(t + 1, 1 - par)
                    act.wait_ge(tr, t + 1)
                    nc.scalar.copy(qkT[:, par, 0:4, :],
                                   ps_t[:, 0, :].rearrange("p (c t) -> p c t", c=4)).then_inc(trq, 1)
                    nc.scalar.copy(uT[:, :, ds(MAXW + t * P, P)],
                                   ps_t[:, 2, :].rearrange("p (c t) -> p c t", c=4)).then_inc(tru, 1)
                    store(t, i, par)
            groups(TILES // 2, 0, psamp[:, :])

        @block.vector
        def _(dve):
            nc.vector.memset(uT[:, :, 0:MAXW], 0.0)

            def x_out(t, par):
                dve.wait_ge(x_read, t + 1)
                nc.vector.tensor_copy(xT[:, par, 4:8, :],
                                      ps_x[:, 1, :].rearrange("p (c t) -> p c t", c=4)).then_inc(xT_dve, 1)

            def groups(i, par, dst):
                for g in range(NG):
                    n = NG * par + g
                    if n % 2 == 1:
                        dve.wait_ge(proj[1], NG * i + n // 2 + 1)
                        nc.vector.tensor_copy(dst[:, GO[g]:GO[g] + GC[g]], ps_p[:, 1, 0:GC[g]]).then_inc(prow_dve, 1)

            x_out(0, 0)
            with dve.Fori(0, TILES // 2) as i:
                for par in range(2):
                    t = 2 * i + par
                    dve.wait_ge(stored[par], 48 * i)
                    dve.wait_ge(gate_kept, 2 * i)
                    groups(i, par, prow[:, par, :])
                    x_out(t + 1, 1 - par)
                    dve.wait_ge(tr, t + 1)
                    nc.vector.tensor_copy(qkT[:, par, 4:8, :],
                                          ps_t[:, 1, :].rearrange("p (c t) -> p c t", c=4)).then_inc(trk, 1)
            groups(TILES // 2, 0, psamp[:, :])
            dve.wait_ge(tail, 1)
            full = uTs[:, :, :, :]
            for g in range(G):
                nc.vector.tensor_copy(full[:, g, :, MAXW - 1:MAXW - 1 + NT],
                                      ps_t[:, 1, g * S:(g + 1) * S].rearrange("p (b t) -> p b t", b=NB))
                nc.vector.tensor_copy(full[:, g, :, 0:MAXW - 1],
                                      ps_t[:, 2, g * P:g * P + NB * (MAXW - 1)]
                                      .rearrange("p (b t) -> p b t", b=NB)).then_inc(tail_copied, 1)

        @block.gpsimd
        def _(pool):
            with pool.Fori(0, TILES // 2) as i:
                for par in range(2):
                    pool.wait_ge(prow_act, NG * i + (3 if par == 0 else 5))
                    pool.wait_ge(prow_dve, NG * i + (2 if par == 0 else 5))
                    nc.gpsimd.tensor_copy(fgate[:, ds(2 * i + par, 1), :],
                                          prow[:, par, 3 * AW:UO].unsqueeze(1)).then_inc(gate_kept, 1)
            pool.wait_ge(prow_act, NG * 8 + 3)
            pool.wait_ge(prow_dve, NG * 8 + 2)
            nc.gpsimd.tensor_copy(fgate[0:S, TILES, :], psamp[0:S, 3 * AW:UO])


def log1p_terms(nc, link, t, w, w2, acc):
    link(nc.vector.tensor_scalar(acc, t, 2.0, None, ALU.add))
    link(nc.vector.reciprocal(acc, acc))
    link(nc.vector.tensor_tensor(w, t, acc, ALU.mult))
    link(nc.vector.tensor_tensor(w2, w, w, ALU.mult))
    link(nc.vector.tensor_scalar(acc, w2, 1.0 / 17, 1.0 / 15, ALU.mult, ALU.add))
    for n in (13, 11, 9, 7, 5, 3, 1):
        link(nc.vector.tensor_tensor(acc, acc, w2, ALU.mult))
        link(nc.vector.tensor_scalar(acc, acc, 1.0 / n, None, ALU.add))
    link(nc.vector.scalar_tensor_tensor(acc, acc, 2.0, w, ALU.mult, ALU.mult))


def stage_gates_pool(nc, io, sc, persist):
    with ExitStack() as ctx:
        m = Mem(nc, ctx, "B")
        ident, uT, fgate, uTs = persist["ident"], persist["uT"], persist["fgate"], persist["uTs"]
        NF = (TILES + 1) * H
        f = fgate[:, :, :].rearrange("p t h -> p (t h)")
        bias = m.sb("bias", [P, H])
        mag, ex, w, w2, lp, lf = (m.sb(n, [P, NF]) for n in ("mag", "ex", "w", "w2", "lp", "lf"))
        upto = m.sb("upto", [P, P])
        before = m.sb("before", [P, P])
        uptos = m.sb("uptos", [S, S])
        ones = m.sb("ones", [P, P])
        onerow = m.sb("onerow", [H, SEQ])
        tot = m.sb("tot", [P, P])
        cs = m.sb("cs", [P, 2, P])
        css = m.sb("css", [S, H])
        cnt = m.sb("cnt", [P, G, MAXW])
        wp = m.sb("wp", [P, G, P])
        psc = m.sb("psc", [P, G])
        wa, wb = m.sb("wa", [P, MAXW + SEQ]), m.sb("wb", [P, MAXW + SEQ])
        sa, sb_ = m.sb("sa", [P, NB, MAXW - 1 + NT]), m.sb("sb", [P, NB, MAXW - 1 + NT])
        pooled = m.sb("pooled", [P, 2, SEQ + S])
        mixed = m.sb("mixed", [P, 2, SEQ + S])
        ps_c = m.ps("c", [P, 512])
        ps_s = m.ps("s", [P, 512])
        ps_m = m.ps("m", [P, 5, 512])

        consts = m.sem("consts")
        cleared = m.sem("cleared")
        z_ready, ex_ready = m.sem("z_ready"), m.sem("ex_ready")
        lf_ready = m.sem("lf_ready")
        tot_ready, tot_out = m.sem("tot_ready"), m.sem("tot_out")
        c_ready, cs_ready = m.sem("c_ready"), m.sem("cs_ready")
        pooled_ready, mixed_ps, mixed_ready = m.sem("pooled_ready"), m.sem("mixed_ps"), m.sem("mixed_ready")
        stored = m.sem("stored")
        mix_stored = [m.sem("mix_stored0"), m.sem("mix_stored1")]
        chain = m.sem("chain")

        block = ctx.enter_context(nc.Block())
        NCONST = 8

        @block.sync
        def _(sp):
            sp.dma_start(bias[:, :], io["b_f"].partition_broadcast(P).rearrange("p a h -> p (a h)")).then_inc(consts, 16)
            sp.dma_start(upto[:, :], io["c_upto"]).then_inc(consts, 16)
            sp.dma_start(before[:, :], io["c_before"]).then_inc(consts, 16)
            sp.dma_start(uptos[:, :], io["c_uptos"]).then_inc(consts, 16)
            sp.dma_start(cnt[:, :, :], io["c_cnt"]).then_inc(consts, 16)
            sp.dma_start(wp[:, :, :], io["w_pool"][0].rearrange("g c e -> c g e")).then_inc(consts, 16)
            sp.dma_start(psc[:, :], io["pool_scale_t"]).then_inc(consts, 16)
            sp.dma_start(persist["causal"][:, :], io["c_causal"]).then_inc(consts, 16)
            sp.wait_ge(cleared, 1)
            sp.dma_start(sc["aug"][:, 1, :], onerow[:, :]).then_inc(stored, 16)
            sp.dma_start(sc["aug"][:, 2, :], onerow[:, :]).then_inc(stored, 16)
            sp.wait_ge(lf_ready, 1)
            lfv = lf[:, :].rearrange("p (t h) -> p t h", h=H)
            sp.dma_start(io["logf_prompt"].rearrange("(t p) h -> p t h", p=P), lfv[:, 0:TILES, :]).then_inc(stored, 16)
            sp.dma_start(io["logf_sample"], lfv[0:S, TILES, :]).then_inc(stored, 16)
            sp.wait_ge(cs_ready, 2)
            sp.dma_start(sc["aug"][:, 0, :].rearrange("h (t p) -> t h p", p=P), cs[:, 0, :]).then_inc(stored, 16)
            sp.dma_start(sc["aug"][:, 3, :].rearrange("h (t p) -> t h p", p=P), cs[:, 1, :]).then_inc(stored, 16)
            sp.dma_start(sc["negc_s"], css[:, :]).then_inc(stored, 16)
            for g in range(G):
                sp.wait_ge(mixed_ready, g + 1)
                sp.dma_start(sc["poolT"][0:TILES, :, g, :].rearrange("n p t -> p n t"),
                             mixed[:, g % 2, 0:SEQ].rearrange("p (n t) -> p n t", t=P)).then_inc(mix_stored[g % 2], 16)
                sp.dma_start(sc["poolT"][TILES, :, g, 0:S], mixed[:, g % 2, SEQ:]).then_inc(mix_stored[g % 2], 16)
            sp.wait_ge(stored, 16 * 7)
            for k in range(2):
                sp.wait_ge(mix_stored[k], 64)

        @block.vector
        def _(dve):
            link = Link(dve, chain)
            nc.vector.memset(ones[:, :], 1.0)
            nc.vector.memset(onerow[:, :], 1.0).then_inc(cleared, 1)
            dve.wait_ge(consts, 16 * NCONST)
            link(nc.vector.memset(fgate[S:P, TILES, :], 0.0))
            link(nc.vector.tensor_tensor(fgate[:, :, :], fgate[:, :, :],
                                         bias[:, :].unsqueeze(1).to_broadcast([P, TILES + 1, H]), ALU.add))
            link(nc.vector.tensor_scalar(mag[:, :], f, -1.0, None, ALU.mult))
            nc.vector.tensor_tensor(mag[:, :], mag[:, :], f, ALU.max).then_inc(z_ready, 1)
            dve.wait_ge(ex_ready, 1)
            log1p_terms(nc, link, ex[:, :], w[:, :], w2[:, :], lp[:, :])
            nc.vector.scalar_tensor_tensor(lf[:, :], f, 0.0, lp[:, :], ALU.min, ALU.subtract).then_inc(lf_ready, 1)
            dve.wait_ge(tot_ready, 1)
            nc.vector.tensor_copy(tot[:, :], ps_s[:, 0:P]).then_inc(tot_out, 1)
            dve.wait_ge(c_ready, 1)
            nc.vector.tensor_scalar(cs[:, 0, :], ps_c[:, 0:P], 1.0 / SCALE, None, ALU.mult)
            nc.vector.tensor_scalar(cs[:, 1, :], ps_c[:, 0:P], -1.0 / SCALE, None, ALU.mult).then_inc(cs_ready, 1)
            nc.vector.tensor_scalar(css[:, :], ps_s[0:S, P:P + H], -1.0 / SCALE, None, ALU.mult).then_inc(cs_ready, 1)
            n = MAXW + SEQ
            for g in range(G):
                if g >= 1:
                    dve.wait_ge(pooled_ready, g)
                if g >= 2:
                    dve.wait_ge(mixed_ps, g - 1)
                src, srcs = uT[:, g, :], uTs[:, g, :, :]
                for k in range(g + 1):
                    sh = 1 << k
                    dst, dsts = (wa, sa) if k % 2 == 0 else (wb, sb_)
                    lo = 2 * sh - 1
                    nc.vector.tensor_tensor(dst[:, lo:n], src[:, lo:n], src[:, lo - sh:n - sh], ALU.add)
                    link(nc.vector.tensor_tensor(dsts[:, :, lo:], srcs[:, :, lo:],
                                                 srcs[:, :, lo - sh:MAXW - 1 + NT - sh], ALU.add))
                    src, srcs = dst[:, :], dsts[:, :, :]
                link(nc.vector.tensor_tensor(src[:, MAXW:2 * MAXW], src[:, MAXW:2 * MAXW], cnt[:, g, :], ALU.mult))
                nc.vector.scalar_tensor_tensor(pooled[:, g % 2, 0:SEQ], src[:, MAXW:n], 0.5 ** (g + 1),
                                               uT[:, g, MAXW:n], ALU.mult, ALU.subtract)
                nc.vector.scalar_tensor_tensor(
                    pooled[:, g % 2, SEQ:].rearrange("p (b t) -> p b t", b=NB), srcs[:, :, MAXW - 1:],
                    0.5 ** (g + 1), uTs[:, g, :, MAXW - 1:], ALU.mult, ALU.subtract).then_inc(pooled_ready, 1)

        @block.scalar
        def _(act):
            act.wait_ge(z_ready, 1)
            nc.scalar.activation(ex[:, :], mag[:, :], ACT.Exp, scale=-1.0).then_inc(ex_ready, 1)
            for g in range(G):
                act.wait_ge(mixed_ps, g + 1)
                if g >= 2:
                    act.wait_ge(mix_stored[g % 2], 32)
                for k in range(5):
                    n = 512 if k < 4 else S
                    last = nc.scalar.activation(mixed[:, g % 2, k * 512:k * 512 + n], ps_m[:, k, 0:n], ACT.Copy,
                                                scale=psc[:, g:g + 1])
                last.then_inc(mixed_ready, 1)

        @block.tensor
        def _(pe):
            pe.wait_ge(lf_ready, 1)
            nc.tensor.matmul(ps_s[:, 0:P], lf[:, 0:P], ones[:, :], start=True, stop=True).then_inc(tot_ready, 1)
            pe.wait_ge(tot_out, 1)
            nc.tensor.matmul(ps_s[0:S, P:P + H], uptos[:, :], lf[0:S, P:NF], start=True, stop=True)
            nc.tensor.matmul(ps_c[:, 0:P], lf[:, 0:P], upto[:, :], start=True, stop=False)
            nc.tensor.matmul(ps_c[:, 0:P], before[:, :], tot[:, :], start=False, stop=True).then_inc(c_ready, 1)
            for g in range(G):
                pe.wait_ge(pooled_ready, g + 1)
                if g >= 1:
                    pe.wait_ge(mixed_ready, g)
                for k in range(5):
                    n = 512 if k < 4 else S
                    last = nc.tensor.matmul(ps_m[:, k, 0:n], wp[:, g, :], pooled[:, g % 2, k * 512:k * 512 + n],
                                            start=True, stop=True)
                last.then_inc(mixed_ps, 1)


def stage_attention(nc, io, sc, persist):
    order = [(0, q) for q in range(TILES)] + [(1, q) for q in reversed(range(TILES))]
    NR = len(order)
    parts = [(q + 4) // 4 for _, q in order]
    first = [sum(parts[:n]) for n in range(NR)]
    NG = sum(parts)
    assert NG % 4 == 0

    def blocks(n, j):
        return min(4, order[n][1] + 1 - 4 * j)

    with ExitStack() as ctx:
        m = Mem(nc, ctx, "C")
        ident, causal, identb = persist["ident"], persist["causal"], persist["identb"]
        K = HD + 2
        qh, kh = m.sb("qh", [K, 2, SEQ]), m.sb("kh", [K, 2, SEQ])
        v = m.sb("v", [P, TILES, AW])
        row = m.sb("row", [P, 2, SEQ])
        pT = m.sb("pT", [P, 4, 512])
        oh = m.sb("oh", [P, 2, TILES, HD])
        mx = m.sb("mx", [P, 2, 4])
        top, nbias, total, rec = (m.sb(n, [P, 2]) for n in ("top", "nbias", "total", "rec"))
        ps_s = m.ps("s", [P, 4, 512])
        ps_t = m.ps("t", [P, 2, 512])
        ps_o = m.ps("o", [P, 2, 512])

        head_in = [m.sem("head_in0"), m.sem("head_in1")]
        v_in = m.sem("v_in")
        s_done, s_copied = m.sem("s_done"), m.sem("s_copied")
        max_ready, exp_done = m.sem("max_ready"), m.sem("exp_done")
        t_done, t_copied = m.sem("t_done"), m.sem("t_copied")
        pv_done, o_done, o_out = m.sem("pv_done"), m.sem("o_done"), m.sem("o_out")
        stored = [m.sem("stored0"), m.sem("stored1")]
        chain = m.sem("chain")

        block = ctx.enter_context(nc.Block())

        @block.sync
        def _(sp):
            def load(i, par):
                sp.dma_start(qh[0:HD, par, :], sc["qkT"][ds(i, 1), par * HD:(par + 1) * HD, :]
                             .rearrange("a p t -> p (a t)")).then_inc(head_in[par], 16)
                sp.dma_start(kh[0:HD, par, :], sc["qkT"][ds(i + AC, 1), par * HD:(par + 1) * HD, :]
                             .rearrange("a p t -> p (a t)")).then_inc(head_in[par], 16)
                sp.dma_start(qh[HD:K, par, :], sc["aug"][ds(2 * i + par, 1), 0:2, :]
                             .rearrange("a r t -> (a r) t")).then_inc(head_in[par], 16)
                sp.dma_start(kh[HD:K, par, :], sc["aug"][ds(2 * i + par, 1), 2:4, :]
                             .rearrange("a r t -> (a r) t")).then_inc(head_in[par], 16)

            load(0, 0)
            sp.dma_start(v[:, :, :], io["v_prompt"].rearrange("(t p) c -> p t c", p=P)).then_inc(v_in, 16)
            load(0, 1)
            with sp.Fori(1, H // 2) as i:
                sp.wait_ge(s_done, NG * i - NG // 2)
                load(i, 0)
                sp.wait_ge(s_done, NG * i)
                load(i, 1)

        @block.tensor
        def _(pe):
            def logits(i, n):
                par, q = order[n]
                if q == (0 if par == 0 else TILES - 1):
                    pe.wait_ge(head_in[par], 64 * i + 64)
                for j in range(parts[n]):
                    c, w = first[n] + j, blocks(n, j) * P
                    pe.wait_ge(s_copied, NG * i + max(c - 3, 0))
                    bank = ps_s[:, c % 4, :]
                    last = nc.tensor.matmul(bank[:, 0:w], qh[:, par, q * P:(q + 1) * P],
                                            kh[:, par, j * 512:j * 512 + w], start=True, stop=j < parts[n] - 1,
                                            skip_group_check=True)
                    if j == parts[n] - 1:
                        last = nc.tensor.matmul(bank[:, w - P:w], identb[:, :], causal[:, :], start=False,
                                                stop=True, skip_group_check=True)
                    last.then_inc(s_done, 1)

            def transposes(i, n, j):
                c = first[n] + j
                if j == 0:
                    pe.wait_ge(exp_done, NR * i + n + 1)
                pe.wait_ge(t_copied, NG * i + max(c - 1, 0))
                for b in range(blocks(n, j)):
                    last = nc.tensor.transpose(ps_t[:, c % 2, b * P:(b + 1) * P],
                                               row[:, n % 2, (4 * j + b) * P:(4 * j + b + 1) * P], ident[:, :])
                last.then_inc(t_done, 1)

            def times_v(i, n, j):
                c = first[n] + j
                pe.wait_ge(t_copied, NG * i + c + 1)
                if j == 0:
                    pe.wait_ge(o_out, NR * i + max(n - 1, 0))
                for b in range(blocks(n, j)):
                    kb = 4 * j + b
                    last = nc.tensor.matmul(ps_o[:, n % 2, 0:P], pT[:, c % 4, b * P:(b + 1) * P],
                                            v[:, kb, ds(i * P, P)], start=kb == 0, stop=kb == order[n][1])
                last.then_inc(pv_done, 1)

            pe.wait_ge(v_in, 16)
            with pe.Fori(0, H // 2) as i:
                logits(i, 0)
                for n in range(NR):
                    if n + 1 < NR:
                        logits(i, n + 1)
                    transposes(i, n, 0)
                    for j in range(1, parts[n]):
                        transposes(i, n, j)
                        times_v(i, n, j - 1)
                    times_v(i, n, parts[n] - 1)

        @block.vector
        def _(dve):
            link = Link(dve, chain)
            NL = 2 * NR

            def copy_logits(i, n):
                k = n % 2
                dve.wait_ge(t_done, NG * i + (first[n - 2] + parts[n - 2] if n >= 2 else 0))
                for j in range(parts[n]):
                    c, w = first[n] + j, blocks(n, j) * P
                    dve.wait_ge(s_done, NG * i + c + 1)
                    last = nc.vector.tensor_scalar(row[:, k, j * 512:j * 512 + w], ps_s[:, c % 4, 0:w], 1.0, None,
                                                   ALU.mult, ALU.max, accum_out=mx[:, k, j:j + 1])
                    last.then_inc(s_copied, 1)
                dve.wait_ge(s_copied, NG * i + first[n] + parts[n])
                link(nc.vector.reduce_max(top[:, k:k + 1], mx[:, k, 0:parts[n]], AXX))
                nc.vector.tensor_scalar(nbias[:, k:k + 1], top[:, k:k + 1], -SCALE, None, ALU.mult)\
                    .then_inc(max_ready, 1)

            with dve.Fori(0, H // 2) as i:
                link.enter(NL * i)
                copy_logits(i, 0)
                for n in range(NR):
                    par, q = order[n]
                    if n + 1 < NR:
                        copy_logits(i, n + 1)
                    for j in range(parts[n]):
                        c, w = first[n] + j, blocks(n, j) * P
                        dve.wait_ge(t_done, NG * i + c + 1)
                        dve.wait_ge(pv_done, NG * i + max(c - 3, 0))
                        nc.vector.tensor_copy(pT[:, c % 4, 0:w], ps_t[:, c % 2, 0:w]).then_inc(t_copied, 1)
                    k = n % 2
                    dve.wait_ge(exp_done, NR * i + n + 1)
                    link(nc.vector.reciprocal(rec[:, k:k + 1], total[:, k:k + 1]))
                    if n in (0, TILES):
                        dve.wait_ge(stored[par], 16 * i)
                    dve.wait_ge(pv_done, NG * i + first[n] + parts[n])
                    nc.vector.tensor_scalar(oh[:, par, q, :], ps_o[:, k, par * HD:(par + 1) * HD],
                                            rec[:, k:k + 1], None, ALU.mult).then_inc(o_out, 1)

        @block.scalar
        def _(act):
            def store(i, par):
                act.wait_ge(o_out, NR * i + TILES * (par + 1))
                act.dma_start(sc["att"].rearrange("(t p) (h d) -> p h t d", p=P, d=HD)[:, ds(2 * i + par, 1), :, :],
                              oh[:, par, :, :].unsqueeze(1)).then_inc(stored[par], 16)

            with act.Fori(0, H // 2) as i:
                for n in range(NR):
                    k, w = n % 2, (order[n][1] + 1) * P
                    act.wait_ge(max_ready, NR * i + n + 1)
                    nc.scalar.activation(row[:, k, 0:w], row[:, k, 0:w], ACT.Exp, bias=nbias[:, k:k + 1],
                                         scale=SCALE, accum_out=total[:, k:k + 1]).then_inc(exp_done, 1)
                    if n == TILES + 2:
                        store(i, 0)
                store(i, 1)
            for par in range(2):
                act.wait_ge(stored[par], 16 * H // 2)


class Norm:

    def __init__(self, nc, m, gain, shift):
        self.nc, self.gain, self.shift = nc, gain, shift
        self.stats, self.mv = m.sb("stats", [P, 2, 6]), m.sb("mv", [P, 2, 2])
        self.var, self.root, self.inv, self.t1 = (m.sb(n, [P, 2]) for n in ("var", "root", "inv", "t1"))
        self.spare = m.sb("nspare", [P, 1])
        self.var_ready, self.root_ready = m.sem("var_ready"), m.sem("root_ready")
        self.scaled, self.normed, self.gained = m.sem("scaled"), m.sem("normed"), m.sem("gained")

    STEPS = 7

    def vector(self, dve, link, r, n, k, rows):
        nc, mv = self.nc, self.mv
        for h in range(2):
            nc.vector.bn_stats(self.stats[0:rows, h, :], r[:, h * 512:(h + 1) * 512]) if h == 0 else \
                link(nc.vector.bn_stats(self.stats[0:rows, h, :], r[:, h * 512:(h + 1) * 512]))
        nc.vector.memset(self.spare[0:rows, :], 0.0)
        link(nc.vector.bn_aggr(mv[0:rows, k, :], self.stats[0:rows, :, :].rearrange("p a b -> p (a b)")))
        var, root, inv, t1 = (x[0:rows, k:k + 1] for x in (self.var, self.root, self.inv, self.t1))
        nc.vector.tensor_scalar(var, mv[0:rows, k, 1:2], EPS, None, ALU.add).then_inc(self.var_ready, 1)
        dve.wait_ge(self.root_ready, n + 1)
        link(nc.vector.reciprocal(inv, root))
        link(nc.vector.tensor_tensor(t1, inv, inv, ALU.mult))
        link(nc.vector.tensor_tensor(t1, t1, var, ALU.mult))
        link(nc.vector.tensor_scalar(t1, t1, -0.5, 1.5, ALU.mult, ALU.add))
        link(nc.vector.tensor_tensor(inv, inv, t1, ALU.mult))
        nc.vector.tensor_scalar(r, r, mv[0:rows, k, 0:1], inv, ALU.subtract, ALU.mult).then_inc(self.normed, 1)

    def scalar(self, act, n, k, rows):
        act.wait_ge(self.var_ready, n + 1)
        self.nc.scalar.activation(self.root[0:rows, k:k + 1], self.var[0:rows, k:k + 1], ACT.Sqrt)\
            .then_inc(self.root_ready, 1)

    def pool(self, pool, r, n, rows):
        pool.wait_ge(self.normed, n + 1)
        self.nc.gpsimd.tensor_tensor(r, r, self.gain[0:rows, :], ALU.mult).then_inc(self.scaled, 1)
        pool.wait_ge(self.scaled, n + 1)
        self.nc.gpsimd.tensor_tensor(r, r, self.shift[0:rows, :], ALU.add).then_inc(self.gained, 1)


def stage_mix(nc, io, sc, persist, sample):
    tag, rows, tiles, xsrc = ("Ds", S, 1, "x_sample") if sample else ("Dp", P, TILES, "x_prompt")
    with ExitStack() as ctx:
        m = Mem(nc, ctx, tag)
        ident = persist["ident"]
        w = m.sb("w", [P, DC, D])
        gain, shift = m.sb("gain", [P, D]), m.sb("shift", [P, D])
        norm = Norm(nc, m, gain, shift)
        att = m.sb("att", [P, 2, AW])
        xin = m.sb("xin", [P, 2, D])
        eT = m.sb("eT", [P, 2, DC, P])
        r = m.sb("r", [P, 2, D])
        rT = m.sb("rT", [P, 2, DC, P])
        ps_a = m.ps("a", [P, 512])
        ps_y = m.ps("y", [P, 2, 2, 512])
        ps_r = m.ps("r", [P, 2, 512])

        w_in, g_in = m.sem("w_in"), m.sem("g_in")
        x_in = [m.sem("x_in0"), m.sem("x_in1")]
        a_in = [m.sem("a_in0"), m.sem("a_in1")]
        p_in = [m.sem("p_in0"), m.sem("p_in1")]
        a_done, a_copied = m.sem("a_done"), m.sem("a_copied")
        y_done, y_read, x_read = m.sem("y_done"), m.sem("y_read"), m.sem("x_read")
        rT_done, rT_copied = m.sem("rT_done"), m.sem("rT_copied")
        stored = [m.sem("stored0"), m.sem("stored1")]
        chain = m.sem("chain")

        def schedule(fori, step, last):
            step(0, 0, 0, False)
            if tiles > 1:
                with fori(0, tiles // 2 - 1) as i:
                    step(2 * i + 1, i, 1, True)
                    step(2 * i + 2, i + 1, 0, True)
                step(tiles - 1, tiles // 2 - 1, 1, True)
            last(tiles - 1, (tiles - 1) // 2, (tiles - 1) % 2)

        block = ctx.enter_context(nc.Block())

        @block.sync
        def _(sp):
            for c in range(DC):
                sp.dma_start(w[:, c, :], io["w_out"][0, c * P:(c + 1) * P, :]).then_inc(w_in, 16)
            sp.dma_start(gain[:, :], io["ln1_g"].partition_broadcast(P).rearrange("p a d -> p (a d)")).then_inc(g_in, 16)
            sp.dma_start(shift[:, :], io["ln1_b"].partition_broadcast(P).rearrange("p a d -> p (a d)")).then_inc(g_in, 16)

            def load_x(t, par):
                src = io[xsrc].rearrange("b t d -> (b t) d")
                sp.dma_start(xin[0:rows, par, :], src if sample else src[ds(t * P, P), :]).then_inc(x_in[par], 16)

            def load_att(t, par):
                if not sample:
                    sp.dma_start(att[:, par, :], sc["att"][ds(t * P, P), :]).then_inc(a_in[par], 16)

            def load_pool(t, par):
                tile = TILES if sample else t
                sp.dma_start(eT[:, par, AC:DC, 0:rows], sc["poolT"][ds(tile, 1), :, :, 0:rows]
                             .rearrange("n p g t -> (n p) g t")).then_inc(p_in[par], 16)

            for t in range(min(2, tiles)):
                load_att(t, t)
                load_x(t, t)
                load_pool(t, t)
            if tiles > 1:
                with sp.Fori(1, tiles // 2) as i:
                    for par in range(2):
                        t = 2 * i + par
                        sp.wait_ge(a_done, t - 1)
                        load_att(t, par)
                        sp.wait_ge(y_done, t - 1)
                        load_pool(t, par)
                        sp.wait_ge(y_read, t - 1)
                        load_x(t, par)

        @block.tensor
        def _(pe):
            pe.wait_ge(w_in, 16 * DC)

            def normed_transposes(t, par):
                pe.wait_ge(norm.gained, t + 1)
                pe.wait_ge(rT_copied, t)
                for c in range(DC):
                    last = nc.tensor.transpose(ps_r[:, c // 4, (c % 4) * P:(c % 4) * P + rows],
                                               r[0:rows, par, c * P:(c + 1) * P], ident[0:rows, 0:rows])
                last.then_inc(rT_done, 1)

            def att_transposes(t, i, par):
                pe.wait_ge(a_in[par], 16 * i + 16)
                pe.wait_ge(a_copied, t)
                for c in range(AC):
                    last = nc.tensor.transpose(ps_a[:, c * P:(c + 1) * P], att[:, par, c * P:(c + 1) * P], ident[:, :])
                last.then_inc(a_done, 1)

            def step(t, i, par, previous):
                pe.wait_ge(p_in[par], 16 * i + 16)
                pe.wait_ge(a_copied, t + 1)
                if not isinstance(t, int) or t >= 2:
                    pe.wait_ge(y_read, t - 1)
                for h in range(2):
                    for c in range(DC):
                        last = nc.tensor.matmul(ps_y[0:rows, par, h, :], eT[:, par, c, 0:rows],
                                                w[:, c, h * 512:(h + 1) * 512], start=c == 0, stop=c == DC - 1)
                last.then_inc(y_done, 1)
                if not isinstance(t, int) or t < tiles - 1:
                    att_transposes(t + 1, i + par, 1 - par)
                if previous:
                    normed_transposes(t - 1, 1 - par)

            if not sample:
                att_transposes(0, 0, 0)
            schedule(pe.Fori, step, lambda t, i, par: normed_transposes(t, par))

        @block.vector
        def _(dve):
            link = Link(dve, chain)

            def step(t, i, par, previous):
                link.enter(norm.STEPS * t)
                dve.wait_ge(x_in[par], 16 * i + 16)
                dve.wait_ge(y_done, t + 1)
                dve.wait_ge(stored[par], 32 * i)
                row = r[0:rows, par, :]
                for h in range(2):
                    last = nc.vector.scalar_tensor_tensor(row[:, h * 512:(h + 1) * 512], xin[0:rows, par, h * 512:(h + 1) * 512],
                                                          ALPHA, ps_y[0:rows, par, h, :], ALU.mult, ALU.add)
                last.then_inc(y_read, 1)
                dve.wait_ge(y_read, t + 1)
                norm.vector(dve, link, row, t, par, rows)

            schedule(dve.Fori, step, lambda t, i, par: None)

        @block.gpsimd
        def _(pool):
            pool.wait_ge(g_in, 32)
            schedule(pool.Fori, lambda t, i, par, previous: norm.pool(pool, r[0:rows, par, :], t, rows),
                     lambda t, i, par: None)

        @block.scalar
        def _(act):
            def finish(t, i, par):
                act.wait_ge(rT_done, t + 1)
                act.wait_ge(stored[par], 32 * i)
                for h in range(2):
                    last = nc.scalar.copy(rT[:, par, 4 * h:4 * h + 4, 0:rows],
                                          ps_r[:, h, :].rearrange("p (c t) -> p c t", c=4)[:, :, 0:rows])
                last.then_inc(rT_copied, 1)
                act.wait_ge(rT_copied, t + 1)
                row, tile = (SEQ, TILES) if sample else (t * P, t)
                act.dma_start(sc["x1"][ds(row, rows), :], r[0:rows, par, :]).then_inc(stored[par], 16)
                act.dma_start(sc["x1T"][ds(tile, 1), :, :, 0:rows].rearrange("n p c t -> (n p) c t"),
                              rT[:, par, :, 0:rows]).then_inc(stored[par], 16)

            def att_out(t, par):
                act.wait_ge(a_done, t + 1)
                nc.scalar.copy(eT[:, par, 0:AC, :], ps_a[:, :].rearrange("p (c t) -> p c t", c=AC)).then_inc(a_copied, 1)

            def step(t, i, par, previous):
                if not isinstance(t, int) or t < tiles - 1:
                    att_out(t + 1, 1 - par)
                norm.scalar(act, t, par, rows)
                if previous:
                    finish(t - 1, i if par else i - 1, 1 - par)

            if sample:
                nc.scalar.copy(eT[:, 0, 0:AC, 0:rows], persist["attT_s"][:, :, :]).then_inc(a_copied, 1)
            else:
                att_out(0, 0)
            schedule(act.Fori, step, finish)
            for par in range(min(2, tiles)):
                act.wait_ge(stored[par], 32 * ((tiles + 1) // 2))


def stage_prepare(nc, io, sc, persist):
    with ExitStack() as ctx:
        m = Mem(nc, ctx, "E0")
        ident, identb = persist["ident"], persist["identb"]
        q4 = m.sb("q4", [P, 2, AW])
        qT = m.sb("qT", [P, 2, 16, 32])
        qbd = m.sb("qbd", [P, NB, 16, 4, NT])
        ks = m.sb("ks", [32, 2, AW])
        kT = m.sb("kT", [32, 2, 16, 32])
        ncs = m.sb("ncs", [32, 2, 32])
        ncT = m.sb("ncT", [32, 2, 32])
        sel = m.sb("sel", [32, 2, P])
        nmask = m.sb("nmask", [P, 32], BF16)
        rowmask = m.sb("rowmask", [P, NB])
        ids = m.sb("ids", [P, 4], I32)
        later, latep = m.sb("later", [P, P]), m.sb("latep", [P, P])
        ones = m.sb("ones", [P, P])
        lin = m.sb("lin", [P, 2, PAGE * H])
        lT = m.sb("lT", [P, H, P])
        tot = m.sb("tot", [P, H])
        rest = m.sb("rest", [P, H, P])
        wn = m.sb("wn", [P, P, 32])
        wT = m.sb("wT", [P, P * 32])
        ps_n = m.ps("n", [P, 2, 2, 32])
        ps_l = m.ps("l", [P, 2, 512])
        ps_w = m.ps("w", [P, 2, 512])

        cin, qin = m.sem("cin"), m.sem("qin")
        zero = m.sem("zero")
        l_in = [m.sem("l_in0"), m.sem("l_in1")]
        qT_ready, kT_ready, n_done, n_read = m.sem("qT_ready"), m.sem("kT_ready"), m.sem("n_done"), m.sem("n_read")
        qbd_ready = m.sem("qbd_ready")
        l_done, l_copied, rest_ready = m.sem("l_done"), m.sem("l_copied"), m.sem("rest_ready")
        w_done, w_copied, wT_ready = m.sem("w_done"), m.sem("w_copied"), m.sem("wT_ready")
        stored, q_stored = m.sem("stored"), m.sem("q_stored")
        chain = m.sem("chain")
        block = ctx.enter_context(nc.Block())

        @block.sync
        def _(sp):
            for dst, name in ((sel[:, :, :], "c_seln"), (nmask[:, :], "c_nmask"), (rowmask[:, :], "c_rowmask"),
                              (later[:, :], "c_later"), (latep[:, :], "c_latep"), (ids[:, :], "page_rows")):
                sp.dma_start(dst, io[name]).then_inc(cin, 16)
            for b in range(4):
                sp.dma_start(q4[b * 32:(b + 1) * 32, :, :], sc["q_s"].rearrange("(g r) c -> r g c", g=2)).then_inc(qin, 16)
            sp.dma_start(ks[:, :, :], io["k_sample"].rearrange("(g r) c -> r g c", g=2)).then_inc(qin, 16)
            for s in range(NB):
                sp.dma_start(sc["vgrp"][s], io["v_sample"][32 * (s // 4):32 * (s // 4) + 32, :]).then_inc(q_stored, 16)
            sp.wait_ge(zero, 1)
            sp.dma_start(ncs[:, :, 0:H], sc["negc_s"].rearrange("(g r) h -> r g h", g=2)).then_inc(qin, 16)
            sp.wait_ge(qbd_ready, 1)
            sp.dma_start(sc["qbd"].rearrange("s p c -> p s c"), qbd[:, :, :, :, :].rearrange("p s f b q -> p s (f b q)"))\
                .then_inc(q_stored, 16)
            with sp.Fori(0, NB // 2) as i:
                sp.wait_ge(wT_ready, i + 1)
                sp.dma_start(sc["wT"][ds(i, 1), :, :].rearrange("a p c -> (a p) c"), wT[:, :]).then_inc(stored, 16)
            sp.wait_ge(stored, 16 * NB // 2)
            sp.wait_ge(q_stored, 16 + 16 * NB)

        @block.gpsimd
        def _(pool):
            pool.wait_ge(cin, 96)
            for i in range(NB // 2):
                if i >= 2:
                    pool.wait_ge(l_done, i - 1)
                    pool.wait_ge(rest_ready, i - 1)
                pool.indirect_dma_start(lin[:, i % 2, :], None, io["cache_logf"],
                                        bass.IndirectOffsetOnAxis(ap=ids[:, i:i + 1], axis=0)).then_inc(l_in[i % 2], 16)

        @block.vector
        def _(dve):
            link = Link(dve, chain)
            nc.vector.memset(ones[:, :], 1.0)
            nc.vector.memset(qbd[:, :, :, :, :], 0.0)
            nc.vector.memset(wn[:, :, :], 0.0)
            nc.vector.memset(ncs[:, :, :], 0.0).then_inc(zero, 1)
            dve.wait_ge(zero, 1)
            dve.wait_ge(cin, 96)
            dve.wait_ge(qin, 96)
            nc.vector.transpose(qT[:, :, :, :], q4[:, :, :].rearrange("p g (f t) -> p g f t", t=32)).then_inc(qT_ready, 1)
            nc.vector.transpose(kT[:, :, :, :], ks[:, :, :].rearrange("p g (f t) -> p g f t", t=32))
            nc.vector.transpose(ncT[:, :, :], ncs[:, :, :]).then_inc(kT_ready, 1)
            dve.wait_ge(qT_ready, 1)
            for b in range(4):
                for g in range(2):
                    part = slice(b * 32, (b + 1) * 32)
                    last = nc.vector.tensor_copy(
                        qbd[part, 4 * g:4 * g + 4, :, b, :].rearrange("p s f q -> p f s q"),
                        qT[part, g, :, :].rearrange("p f (s q) -> p f s q", s=4))
            last.then_inc(qbd_ready, 1)
            dve.wait_ge(n_done, 1)
            for s in range(NB):
                last = nc.vector.tensor_scalar(persist["snew"][:, s, :, :], ps_n[:, s // 4, :, :],
                                               rowmask[:, s:s + 1], None, ALU.add)
            last.then_inc(n_read, 1)
            for i in range(NB // 2):
                dve.wait_ge(l_in[i % 2], 16 * (i // 2 + 1))
                if i:
                    dve.wait_ge(w_done, i)
                link(nc.vector.reduce_sum(tot[:, :], lin[:, i % 2, :].rearrange("p (t h) -> p h t", h=H), AXX))
                nc.vector.tensor_tensor(rest[:, :, :], latep[:, :].unsqueeze(1).to_broadcast([P, H, P]),
                                        tot[:, :].unsqueeze(2).to_broadcast([P, H, P]), ALU.mult).then_inc(rest_ready, 1)
                dve.wait_ge(rest_ready, i + 1)
                dve.wait_ge(l_done, i + 1)
                for h in range(2):
                    last = nc.vector.tensor_copy(lT[:, 4 * h:4 * h + 4, :], ps_l[:, h, :].rearrange("p (h g) -> p h g", h=4))
                last.then_inc(l_copied, 1)
                dve.wait_ge(w_done, i + 1)
                if i:
                    dve.wait_ge(stored, 16 * i)
                for h in range(2):
                    last = nc.vector.tensor_scalar(wn[:, :, 4 * h:4 * h + 4].rearrange("p g h -> p h g"),
                                                   ps_w[:, h, :].rearrange("p (h g) -> p h g", h=4), 1.0 / SCALE, None, ALU.mult)
                last.then_inc(w_copied, 1)
                dve.wait_ge(w_copied, i + 1)
                nc.vector.transpose(wT[:, :], wn[:, :, :].rearrange("p g h -> p (g h)")).then_inc(wT_ready, 1)
                dve.wait_ge(wT_ready, i + 1)

        @block.tensor
        def _(pe):
            pe.wait_ge(cin, 96)
            pe.wait_ge(qT_ready, 1)
            pe.wait_ge(kT_ready, 1)
            for g in range(2):
                for st in range(2):
                    out = ps_n[:, g, st, :]
                    nc.tensor.matmul(out, sel[:, st, :], ncT[:, g, :], start=True, stop=False, skip_group_check=True)
                    nc.tensor.matmul(out, identb[:, :], nmask[:, :], start=False, stop=False, skip_group_check=True)
                    for half in range(2):
                        for hs in range(4):
                            f = 2 * (4 * st + hs) + half
                            last = nc.tensor.matmul(out[32 * hs:32 * hs + 32, :], qT[0:32, g, f, :], kT[:, g, f, :],
                                                    start=False, stop=half == 1, skip_group_check=True)
            last.then_inc(n_done, 1)
            for i in range(NB // 2):
                pe.wait_ge(l_in[i % 2], 16 * (i // 2 + 1))
                if i:
                    pe.wait_ge(l_copied, i)
                lv = lin[:, i % 2, :].rearrange("p (t h) -> p h t", h=H)
                for h in range(H):
                    last = nc.tensor.transpose(ps_l[:, h // 4, (h % 4) * P:(h % 4 + 1) * P], lv[:, h, :], ident[:, :])
                last.then_inc(l_done, 1)
                pe.wait_ge(l_copied, i + 1)
                pe.wait_ge(rest_ready, i + 1)
                if i:
                    pe.wait_ge(w_copied, i)
                for h in range(2):
                    nc.tensor.matmul(ps_w[:, h, :], later[:, :], lT[:, 4 * h:4 * h + 4, :].rearrange("p h g -> p (h g)"),
                                     start=True, stop=False)
                    last = nc.tensor.matmul(ps_w[:, h, :], ones[:, :], rest[:, 4 * h:4 * h + 4, :].rearrange("p h g -> p (h g)"),
                                            start=False, stop=True)
                last.then_inc(w_done, 1)


class Decode:

    PARTS = 17
    UN = NPG // 4
    NBUF = 4

    def __init__(self, nc, m, io, sc, persist):
        self.nc, self.io, self.sc, self.persist = nc, io, sc, persist
        self.kin, self.kt = m.sb("kin", [P, self.NBUF, 4, AW]), m.sb("kt", [P, 2, 16, P])
        self.vin = m.sb("vin", [P, self.NBUF, 4, AW])
        self.vnew = m.sb("vnew", [32, 2, AW])
        self.qbd, self.wT = m.sb("qbd", [P, 2, 16, 32]), m.sb("wT", [P, 2, NPG * 32])
        self.logits = m.sb("logits", [P, 2, 2, NPG * 32 + 32])
        self.ecur, self.enew = m.sb("ecur", [P, 2, 2, P]), m.sb("enew", [P, 2, 32])
        self.pt, self.ptn = m.sb("pt", [P, 2, 2, 4, 32]), m.sb("ptn", [32, 2, 32])
        self.nbias, self.sums = m.sb("nbias", [P, 2, 2]), m.sb("sums", [P, 2, 2, self.PARTS])
        self.mx, self.mxb, self.mxe = m.sb("mx", [P, 2]), m.sb("mxb", [2, 32]), m.sb("mxe", [P, P])
        self.lp, self.rec, self.osb = m.sb("lp", [P, 2]), m.sb("rec", [P, 1]), m.sb("osb", [P, 2 * P])
        self.sel, self.lsel, self.osel = m.sb("sel", [P, 2, P]), m.sb("lsel", [P, 2, P]), m.sb("osel", [P, AC, 16])
        self.ids = m.sb("ids", [1, NB * NPG], I32)
        self.zero = m.sb("zero", [P, 2 * P])
        self.ps_s = m.ps("s", [P, 2, 512])
        self.ps_t = m.ps("t", [P, 512])
        self.ps_o = m.ps("o", [P, 512])
        sem = m.sem
        self.cin = sem("cin")
        self.k_in, self.v_in = ([sem(f"{n}{i}") for i in range(self.NBUF)] for n in ("k_in", "v_in"))
        self.seq_in = [sem("seq_in0"), sem("seq_in1")]
        self.k_turned, self.s_done, self.s_copied, self.exp_done = sem("k_turned"), sem("s_done"), sem("s_copied"), sem("exp_done")
        self.t_done, self.t_copied, self.pv_done = sem("t_done"), sem("t_copied"), sem("pv_done")
        self.max_pe, self.max_dve, self.mxb_ready = sem("max_pe"), sem("max_dve"), sem("mxb_ready")
        self.out_pe, self.out_dve, self.lp_ready = sem("out_pe"), sem("out_dve"), sem("lp_ready")
        self.copied_new = sem("copied_new")
        self.top_ready = sem("top_ready")
        self.rec_ready = sem("rec_ready")

    def consts(self, sp):
        for dst, name in ((self.sel[:, :, :], "c_sel"), (self.lsel[:, :, :], "c_lsel"), (self.osel[:, :, :], "c_osel"),
                          (self.ids[:, :], "page_ids")):
            sp.dma_start(dst, self.io[name]).then_inc(self.cin, 16)

    def load_seq(self, sp, s, i2, sp_):
        if not isinstance(s, int) or s >= 2:
            sp.wait_ge(self.s_done, 2 + self.UN * (s - 1))
            sp.wait_ge(self.pv_done, 2 + self.PARTS * (s - 2) + 1)
        sp.dma_start(self.qbd[:, sp_, :, :], self.sc["qbd"][ds(s, 1), :, :].rearrange("a p (f c) -> (a p) f c", f=16))\
            .then_inc(self.seq_in[sp_], 16)
        sp.dma_start(self.vnew[:, sp_, :], self.sc["vgrp"][ds(s, 1), :, :].rearrange("a t c -> (a t) c"))\
            .then_inc(self.seq_in[sp_], 16)
        sp.dma_start(self.wT[:, sp_, :], self.sc["wT"][ds(i2, 1), :, sp_ * 2048:(sp_ + 1) * 2048]
                     .rearrange("a p c -> (a p) c")).then_inc(self.seq_in[sp_], 16)

    def load_k(self, sp, s, u, buf):
        n = self.UN * s + u
        _, pages = self.nc.values_load_multi_w_load_instructions(
            self.ids[0:1, ds(4 * n, 4)], engines=(mybir.EngineType.SP,), min_val=0, max_val=NPOOL - 1)
        sp.wait_ge(self.k_turned, n + 1)
        for j in range(4):
            sp.dma_start(self.kin[:, buf, j, :], self.io["cache_k"][ds(pages[j], 1), :, :].rearrange("a t c -> (a t) c"))\
                .then_inc(self.k_in[buf], 16)

    def load_v(self, sp, s, u, buf):
        n = self.UN * s + u
        _, pages = self.nc.values_load_multi_w_load_instructions(
            self.ids[0:1, ds(4 * n, 4)], engines=(mybir.EngineType.SP,), min_val=0, max_val=NPOOL - 1)
        sp.wait_ge(self.pv_done, self.PARTS * s + u)
        for j in range(4):
            sp.dma_start(self.vin[32 * j:32 * j + 32, buf, :, :],
                         self.io["cache_v"][ds(pages[j], 1), :, :].rearrange("a (b t) c -> (a t) b c", b=4))\
                .then_inc(self.v_in[buf], 16)

    def credits(self, dve):
        nc = self.nc
        nc.vector.memset(self.mx[:, :], 0.0).then_inc(self.k_turned, 4)
        nc.vector.memset(self.lp[:, :], 0.0).then_inc(self.s_done, 2)
        nc.vector.memset(self.rec[:, :], 0.0).then_inc(self.s_copied, 2)
        nc.vector.memset(self.enew[:, :, :], 0.0).then_inc(self.exp_done, self.PARTS)
        nc.vector.memset(self.osb[:, :], 0.0).then_inc(self.pv_done, 2)

    def turn_k(self, dve, s, u, turn, buf, par):
        n = self.UN * s + u
        dve.wait_ge(self.k_in[buf], 64 * turn + 64)
        dve.wait_ge(self.s_done, n + 1)
        self.nc.vector.transpose(self.kt[:, par, :, :].rearrange("p f (j t) -> p j f t", j=4),
                                 self.kin[:, buf, :, :].rearrange("p j (f t) -> p j f t", t=32)).then_inc(self.k_turned, 1)

    def copy_pt(self, dve, s, u, par):
        c = self.PARTS * s + u + 1
        dve.wait_ge(self.t_done, c + 1)
        dve.wait_ge(self.pv_done, c + 1)
        self.nc.vector.tensor_copy(self.pt[:, par, :, :, :].rearrange("p s b (h q) -> p s h b q", h=4),
                                   self.ps_t[:, 0:2 * P].rearrange("p (s h b q) -> p s h b q", s=2, h=4, b=4))\
            .then_inc(self.t_copied, 1)

    def maximum(self, dve, s, sp_):
        nc, lg = self.nc, self.logits
        dve.wait_ge(self.exp_done, self.PARTS * s)
        nc.vector.tensor_copy(lg[:, sp_, :, NPG * 32:], self.persist["snew"][:, ds(s, 1), :, :]
                              .rearrange("p a s k -> p (a s) k")).then_inc(self.copied_new, 1)
        dve.wait_ge(self.copied_new, s + 1)
        dve.wait_ge(self.s_copied, 2 + self.UN * s + self.UN)
        dve.wait_ge(self.max_pe, 2 * s)
        nc.vector.reduce_max(self.mx[:, :], lg[:, sp_, :, :], AXX).then_inc(self.top_ready, 1)
        dve.wait_ge(self.max_pe, 2 * s + 1)
        nc.vector.reduce_max(self.mxb[:, :].rearrange("s (h q) -> s h q", h=4),
                             self.ps_t[0:2, 0:P].rearrange("s (h b q) -> s h q b", h=4, b=4), AXX).then_inc(self.mxb_ready, 1)
        dve.wait_ge(self.mxb_ready, s + 1)
        nc.vector.tensor_copy(self.mxe[0:2, :].rearrange("s (h b q) -> s h b q", h=4, b=4),
                              self.mxb[:, :].rearrange("s (h q) -> s h q", h=4).unsqueeze(2).to_broadcast([2, 4, 4, NT]))\
            .then_inc(self.max_dve, 1)
        dve.wait_ge(self.max_pe, 2 * s + 2)
        nc.vector.tensor_scalar(self.nbias[:, sp_, :], self.ps_t[:, P:P + 2], -SCALE, None, ALU.mult).then_inc(self.max_dve, 1)

    def new_pt(self, dve, s):
        dve.wait_ge(self.t_done, self.PARTS * s + 1)
        dve.wait_ge(self.pv_done, 2 + self.PARTS * s)
        self.nc.vector.reduce_sum(self.ptn[:, :, :].rearrange("k s (h q) -> k s h q", h=4),
                                  self.ps_t[0:32, 0:2 * P].rearrange("k (s h b q) -> k s h q b", s=2, h=4, b=4), AXX)\
            .then_inc(self.t_copied, 1)

    def finish_dve(self, dve, s, sp_):
        nc = self.nc
        dve.wait_ge(self.exp_done, self.PARTS * (s + 2))
        dve.wait_ge(self.out_pe, 2 * s)
        nc.vector.reduce_sum(self.lp[:, :], self.sums[:, sp_, :, :], AXX).then_inc(self.lp_ready, 1)
        dve.wait_ge(self.out_pe, 2 * s + 1)
        nc.vector.reciprocal(self.rec[:, :], self.ps_t[:, 2 * P:2 * P + 1]).then_inc(self.rec_ready, 1)
        dve.wait_ge(self.rec_ready, s + 1)
        nc.vector.tensor_scalar(self.osb[:, :], self.ps_o[:, 0:2 * P], self.rec[:, 0:1], None, ALU.mult).then_inc(self.out_dve, 1)
        dve.wait_ge(self.out_pe, 2 * s + 2)
        for hh in range(2):
            part = slice(64 * hh, 64 * hh + 64)
            last = nc.vector.tensor_copy(self.persist["attT_s"][part, :, ds(NT * s, NT)],
                                         self.ps_t[part, 2 * P + 16:2 * P + 80].rearrange("p (c e) -> p c e", c=AC)
                                         [:, :, NT * hh:NT * hh + NT])
        last.then_inc(self.out_dve, 1)

    def exp(self, act, s, u, par, sp_):
        if isinstance(u, int) and u == 0:
            raise ValueError
        act.wait_ge(self.t_done, self.PARTS * s + u)
        for st in range(2):
            last = self.nc.scalar.activation(self.ecur[:, par, st, :], self.logits[:, sp_, st, ds(u * P, P)], ACT.Exp,
                                             bias=self.nbias[:, sp_, st:st + 1], scale=SCALE,
                                             accum_out=self.sums[:, sp_, st, ds(u + 1, 1)])
        last.then_inc(self.exp_done, 1)

    def exp_new(self, act, s, sp_):
        act.wait_ge(self.max_dve, 2 * s + 2)
        act.wait_ge(self.t_done, self.PARTS * s)
        if not isinstance(s, int) or s >= 1:
            act.wait_ge(self.lp_ready, s - 1)
        for st in range(2):
            last = self.nc.scalar.activation(self.enew[:, st, :], self.logits[:, sp_, st, NPG * 32:], ACT.Exp,
                                             bias=self.nbias[:, sp_, st:st + 1], scale=SCALE,
                                             accum_out=self.sums[:, sp_, st, 0:1])
        last.then_inc(self.exp_done, 1)

    def copy_s(self, act, s, u, par, sp_):
        n = self.UN * s + u
        act.wait_ge(self.exp_done, self.PARTS * s)
        act.wait_ge(self.s_done, n + 3)
        self.nc.scalar.copy(self.logits[:, sp_, :, ds(u * P, P)],
                            self.ps_s[:, par, 0:2 * P].rearrange("p (s k) -> p s k", s=2)).then_inc(self.s_copied, 1)

    def seq_ready(self, pe, s, i2, sp_):
        pe.wait_ge(self.seq_in[sp_], 48 * i2 + 48)

    def qk(self, pe, s, u, par, sp_):
        n, nc = self.UN * s + u, self.nc
        pe.wait_ge(self.k_turned, n + 5)
        pe.wait_ge(self.s_copied, n + 1)
        for st in range(2):
            out = self.ps_s[:, par, st * P:(st + 1) * P]
            nc.tensor.matmul(out, self.sel[:, st, :], self.wT[:, sp_, ds(u * P, P)], start=True, stop=False,
                             skip_group_check=True)
            for half in range(2):
                for hs in range(4):
                    f = 2 * (4 * st + hs) + half
                    last = nc.tensor.matmul(out[32 * hs:32 * hs + 32, :], self.qbd[:, sp_, f, :], self.kt[:, par, f, :],
                                            start=False, stop=half == 1, skip_group_check=True)
        last.then_inc(self.s_done, 1)

    def transpose_p(self, pe, s, u, par):
        c, nc = self.PARTS * s + u + 1, self.nc
        pe.wait_ge(self.exp_done, self.PARTS + c + 1)
        pe.wait_ge(self.t_copied, c)
        for st in range(2):
            last = nc.tensor.transpose(self.ps_t[:, st * P:(st + 1) * P], self.ecur[:, par, st, :], self.persist["ident"][:, :])
        last.then_inc(self.t_done, 1)

    def pv(self, pe, s, u, turn, buf, par):
        c, nc = self.PARTS * s + u + 1, self.nc
        pe.wait_ge(self.t_copied, c + 1)
        pe.wait_ge(self.v_in[buf], 64 * turn + 64)
        for b in range(4):
            for st in range(2):
                row = 64 * st + 32 * (b % 2)
                last = nc.tensor.matmul(self.ps_o[row:row + 32, 0:2 * P], self.pt[:, par, st, b, :],
                                        self.vin[:, buf, b, st * 2 * P:(st + 1) * 2 * P], start=False, stop=False,
                                        skip_group_check=True)
        last.then_inc(self.pv_done, 1)

    def maximum_pe(self, pe, s):
        nc, ident = self.nc, self.persist["ident"]
        pe.wait_ge(self.top_ready, s + 1)
        nc.tensor.transpose(self.ps_t[0:2, 0:P], self.mx[:, :], ident[:, :]).then_inc(self.max_pe, 1)
        pe.wait_ge(self.max_dve, 2 * s + 1)
        nc.tensor.transpose(self.ps_t[:, P:2 * P], self.mxe[:, :], ident[:, :]).then_inc(self.max_pe, 1)

    def new_tokens_pe(self, pe, s, sp_):
        nc, c = self.nc, self.PARTS * s
        pe.wait_ge(self.exp_done, self.PARTS + c + 1)
        pe.wait_ge(self.max_dve, 2 * s + 2)
        for st in range(2):
            last = nc.tensor.transpose(self.ps_t[0:32, st * P:(st + 1) * P], self.enew[:, st, :], self.persist["ident"][:, :])
        last.then_inc(self.t_done, 1)
        pe.wait_ge(self.t_copied, c + 1)
        nc.tensor.matmul(self.ps_o[:, 0:2 * P], self.zero[:, 0:P], self.zero[:, :], start=True, stop=False,
                         skip_group_check=True)
        for st in range(2):
            last = nc.tensor.matmul(self.ps_o[64 * st:64 * st + 32, 0:2 * P], self.ptn[:, st, :],
                                    self.vnew[:, sp_, st * 2 * P:(st + 1) * 2 * P], start=False, stop=False,
                                    skip_group_check=True)
        last.then_inc(self.pv_done, 1)

    def finish_pe(self, pe, s):
        nc = self.nc
        pe.wait_ge(self.lp_ready, s + 1)
        pe.wait_ge(self.t_copied, self.PARTS * (s + 1))
        for st in range(2):
            last = nc.tensor.matmul(self.ps_t[:, 2 * P:2 * P + 1], self.lsel[:, st, :], self.lp[:, st:st + 1],
                                    start=st == 0, stop=st == 1)
        last.then_inc(self.out_pe, 1)
        pe.wait_ge(self.out_dve, 2 * s + 1)
        for c in range(AC):
            last = nc.tensor.matmul(self.ps_t[:, 2 * P + 16 + 16 * c:2 * P + 32 + 16 * c],
                                    self.osb[:, (c % 2) * P:(c % 2 + 1) * P], self.osel[:, c, :], start=True, stop=True)
        last.then_inc(self.out_pe, 1)
        pe.wait_ge(self.out_dve, 2 * s + 2)


def stage_decode(nc, io, sc, persist):
    with ExitStack() as ctx:
        m = Mem(nc, ctx, "E")
        d = Decode(nc, m, io, sc, persist)
        zeroed = m.sem("zeroed")
        block = ctx.enter_context(nc.Block())
        TURNS = d.UN // d.NBUF

        def run(fori, k_step, v_step, boundary):
            def seq(s, i2, sp_, k, v):
                with fori(0, TURNS) as j:
                    for buf in range(d.NBUF):
                        u, par = d.NBUF * j + buf, buf % 2
                        if v:
                            v_step(0, s - 1, u, TURNS * (s - 1) + j, buf, par, 1 - sp_)
                        if k:
                            k_step(s, u, TURNS * s + j, buf, par, sp_)
                        if v:
                            v_step(1, s - 1, u, TURNS * (s - 1) + j, buf, par, 1 - sp_)
                boundary(s, i2, sp_, k, v)

            seq(0, 0, 0, True, False)
            with fori(0, NB // 2 - 1) as i:
                seq(2 * i + 1, i, 1, True, True)
                seq(2 * i + 2, i + 1, 0, True, True)
            seq(NB - 1, NB // 2 - 1, 1, True, True)
            seq(NB, NB // 2, 0, False, True)

        @block.sync
        def _(sp):
            d.consts(sp)
            d.load_seq(sp, 0, 0, 0)
            sp.wait_ge(d.cin, 64)

            def k_step(s, u, turn, buf, par, sp_):
                d.load_k(sp, s, u, buf)

            def v_step(half, s, u, turn, buf, par, sp_):
                if half == 1:
                    d.load_v(sp, s, u, buf)

            def boundary(s, i2, sp_, k, v):
                if k and not (isinstance(s, int) and s + 1 >= NB):
                    d.load_seq(sp, s + 1, i2 + sp_, 1 - sp_)

            run(sp.Fori, k_step, v_step, boundary)

        @block.vector
        def _(dve):
            d.credits(dve)
            nc.vector.memset(d.mxe[:, :], 0.0).then_inc(zeroed, 1)
            dve.wait_ge(zeroed, 1)
            nc.vector.memset(d.zero[:, :], 0.0).then_inc(zeroed, 1)

            def v_step(half, s, u, turn, buf, par, sp_):
                if half == 1:
                    d.copy_pt(dve, s, u, par)

            def boundary(s, i2, sp_, k, v):
                if v:
                    d.finish_dve(dve, s - 1, 1 - sp_)
                if k:
                    d.maximum(dve, s, sp_)
                    d.new_pt(dve, s)

            run(dve.Fori, lambda s, u, turn, buf, par, sp_: d.turn_k(dve, s, u, turn, buf, par), v_step, boundary)

        @block.scalar
        def _(act):
            def v_step(half, s, u, turn, buf, par, sp_):
                if half == 0:
                    d.exp(act, s, u, par, sp_)

            def boundary(s, i2, sp_, k, v):
                if k:
                    d.exp_new(act, s, sp_)

            run(act.Fori, lambda s, u, turn, buf, par, sp_: d.copy_s(act, s, u, par, sp_), v_step, boundary)

        @block.tensor
        def _(pe):
            pe.wait_ge(d.cin, 64)
            pe.wait_ge(zeroed, 2)
            d.seq_ready(pe, 0, 0, 0)

            def v_step(half, s, u, turn, buf, par, sp_):
                if half == 0:
                    d.transpose_p(pe, s, u, par)
                else:
                    d.pv(pe, s, u, turn, buf, par)

            def boundary(s, i2, sp_, k, v):
                if v:
                    d.finish_pe(pe, s - 1)
                if k:
                    d.maximum_pe(pe, s)
                    if not isinstance(s, int) or s + 1 < NB:
                        d.seq_ready(pe, s + 1, i2 + sp_, 1 - sp_)
                    d.new_tokens_pe(pe, s, sp_)

            run(pe.Fori, lambda s, u, turn, buf, par, sp_: d.qk(pe, s, u, par, sp_), v_step, boundary)


def stage_ffn(nc, io, sc, persist, sample):
    tag, seqs, T, blocks, tiles, rows, y = ("Fs", NB, NT, 1, 1, S, "y_sample") if sample else \
        ("Fp", 1, TB, BLOCKS, TB // P, P, "y_prompt")
    N = seqs * T
    state = "conv_sample" if sample else "conv_prompt"
    WG = 2
    LOADS = 2 * FC // WG
    with ExitStack() as ctx:
        m = Mem(nc, ctx, tag)
        gain, shift = m.sb("gain", [P, D]), m.sb("shift", [P, D])
        norm = Norm(nc, m, gain, shift)
        xT = m.sb("xT", [P, DC, N])
        r = m.sb("r", [P, tiles, D])
        wu = m.sb("wu", [P, 2, 2, DC, P])
        coef = m.sb("coef", [P, 2, 2, 5])
        h = m.sb("h", [P, 2, 2, seqs, 2 + T])
        cv = m.sb("cv", [P, 2, 2, N])
        gT = m.sb("gT", [P, FC, N])
        hist = m.sb("hist", [P, FC, 2, seqs, 2])
        wd = m.sb("wd", [P, 2, WG, 512])
        zero, spare = m.sb("zero", [P, 1]), m.sb("spare", [P, 1])
        ps = m.ps("u", [P, 2, 2, 512])

        g_in, x_in, r_in, s_in = m.sem("g_in"), m.sem("x_in"), m.sem("r_in"), m.sem("s_in")
        wu_in = [m.sem("wu_in0"), m.sem("wu_in1")]
        wd_in = [m.sem("wd_in0"), m.sem("wd_in1")]
        up_done, up_out, conv_read, tails, down_done = (m.sem(n) for n in ("up_done", "up_out", "conv_read", "tails", "down_done"))
        halos, gate_ready, gelu_done, gT_ready = (m.sem(n) for n in ("halos", "gate_ready", "gelu_done", "gT_ready"))
        y_read, stored, chain, norm_chain = (m.sem(n) for n in ("y_read", "stored", "chain", "norm_chain"))
        hist_ready, state_out = m.sem("hist_ready"), m.sem("state_out")

        def over_blocks(eng, body):
            if blocks == 1:
                body(0)
            else:
                with eng.Fori(0, blocks) as b:
                    body(b)

        def over_chunks(eng, b, body):
            with eng.Fori(0, FC // 2) as j:
                for par in range(2):
                    body(2 * j + par, FC * b + (2 * j + par), FC // 2 * b + j, par)

        block = ctx.enter_context(nc.Block())

        @block.sync
        def _(sp):
            sp.dma_start(gain[:, :], io["ln2_g"].partition_broadcast(P).rearrange("p a d -> p (a d)")).then_inc(g_in, 16)
            sp.dma_start(shift[:, :], io["ln2_b"].partition_broadcast(P).rearrange("p a d -> p (a d)")).then_inc(g_in, 16)
            if sample:
                sp.dma_start(hist[:, :, :, :, :], io["state_conv_t"]).then_inc(s_in, 16)

            def body(b):
                sp.wait_ge(up_done, 4 + 2 * FC * b)
                for k in range(tiles):
                    tile = TILES if sample else tiles * b + k
                    sp.dma_start(xT[:, :, k * P:k * P + rows], sc["x1T"][ds(tile, 1), :, :, 0:rows]
                                 .rearrange("n p c t -> (n p) c t")).then_inc(x_in, 16)

                def chunk(f, n, turn, par):
                    sp.wait_ge(up_done, 2 * n + 2)
                    sp.dma_start(wu[:, par, :, :, :], io["w_up_t"][ds(f, 1), :, :, :, :]
                                 .rearrange("f p g c k -> (f p) g c k")).then_inc(wu_in[par], 16)
                    sp.wait_ge(conv_read, n + 1)
                    sp.dma_start(coef[:, par, :, :], io["coef_t"][ds(f, 1), :, :, :]
                                 .rearrange("f p g k -> (f p) g k")).then_inc(wu_in[par], 16)

                over_chunks(sp, b, chunk)
                sp.wait_ge(stored, 16 * tiles * b)
                for k in range(tiles):
                    src = sc["x1"][SEQ:SEQ + S, :] if sample else sc["x1"][ds(TB * b + k * P, P), :]
                    sp.dma_start(r[0:rows, k, :], src).then_inc(r_in, 16)
                for half in range(2):
                    for g in range(FC // WG):
                        n = half * (FC // WG) + g
                        sp.wait_ge(down_done, LOADS * b + n + 1)
                        sp.dma_start(wd[:, n % 2, :, :], io["w_down"][0, g * WG * P:(g + 1) * WG * P, half * 512:(half + 1) * 512]
                                     .rearrange("(g p) d -> p g d", p=P)).then_inc(wd_in[n % 2], 16)

            over_blocks(sp, body)
            sp.wait_ge(tails, 2 + FC * blocks)
            sp.dma_start(io[state], hist[:, :, :, :, :]).then_inc(state_out, 16)
            sp.wait_ge(state_out, 16)
            sp.wait_ge(stored, 16 * tiles * blocks)

        @block.tensor
        def _(pe):
            def body(b):
                def chunk(f, n, turn, par):
                    pe.wait_ge(x_in, 16 * tiles * (b + 1))
                    pe.wait_ge(y_read, 2 * tiles * b)
                    pe.wait_ge(wu_in[par], 32 * turn + 32)
                    for gv in range(2):
                        pe.wait_ge(up_out, 2 * n + gv + 1)
                        for c in range(DC):
                            last = nc.tensor.matmul(ps[:, par, gv, 0:N], wu[:, par, gv, c, :], xT[:, c, :],
                                                    start=c == 0, stop=c == DC - 1)
                        last.then_inc(up_done, 1)

                over_chunks(pe, b, chunk)
                pe.wait_ge(up_out, 4 + 2 * FC * (b + 1))
                for half in range(2):
                    for f in range(FC):
                        n = half * (FC // WG) + f // WG
                        if f % WG == 0:
                            pe.wait_ge(wd_in[n % 2], 16 * (LOADS // 2 * b + n // 2 + 1))
                        if half == 0:
                            pe.wait_ge(gT_ready, FC * b + f + 1)
                        for k in range(tiles):
                            if f == 0 and half == 1:
                                pe.wait_ge(y_read, 2 * tiles * b + k + 1)
                            last = nc.tensor.matmul(ps[0:rows, k // 2, k % 2, :], gT[:, f, k * P:k * P + rows],
                                                    wd[:, n % 2, f % WG, :], start=f == 0, stop=f == FC - 1,
                                                    skip_group_check=True)
                        if f % WG == WG - 1:
                            last.then_inc(down_done, 1)

            over_blocks(pe, body)

        @block.scalar
        def _(act):
            def body(b):
                def chunk(f, n, turn, par):
                    act.wait_ge(conv_read, n + 1)
                    act.wait_ge(tails, n + 1)
                    for gv in range(2):
                        act.wait_ge(up_done, 4 + 2 * n + gv + 1)
                        nc.scalar.activation(h[:, par, gv, :, 2:2 + T], ps[:, par, gv, 0:N].rearrange("p (s t) -> p s t", s=seqs),
                                             ACT.Identity, bias=coef[:, par, gv, 0:1]).then_inc(up_out, 1)
                    act.wait_ge(gate_ready, n + 1)
                    nc.scalar.activation(cv[:, par, 0, :], cv[:, par, 0, :], ACT.Gelu_apprx_tanh).then_inc(gelu_done, 1)

                over_chunks(act, b, chunk)
                for k in range(tiles):
                    norm.scalar(act, tiles * b + k, k % 2, rows)
                for k in range(tiles):
                    act.wait_ge(norm.gained, tiles * b + k + 1)
                    dst = io[y] if sample else io[y][ds(TB * b + k * P, P), :]
                    act.dma_start(dst, r[0:rows, k, :]).then_inc(stored, 16)

            over_blocks(act, body)

        @block.vector
        def _(dve):
            link, norm_link = Link(dve, chain), Link(dve, norm_chain)
            for sem, n in ((up_done, 4), (up_out, 4), (conv_read, 2), (down_done, 2), (tails, 2)):
                nc.vector.memset(zero[:, :], 0.0).then_inc(sem, n)
                dve.wait_ge(sem, n)
            STEPS = 2

            def body(b):
                def chunk(f, n, turn, par):
                    link.enter(STEPS * n)
                    dve.wait_ge(up_out, 4 + 2 * n + 2)
                    dve.wait_ge(halos, n + 1)
                    dve.wait_ge(gT_ready, n)
                    for tap in range(3):
                        for gv in range(2):
                            src = h[:, par, gv, :, tap:tap + T]
                            dst = cv[:, par, gv, :].rearrange("p (s t) -> p s t", s=seqs)
                            w = coef[:, par, gv, 1 + tap:2 + tap]
                            if tap == 0:
                                last = nc.vector.tensor_scalar(dst, src, w, coef[:, par, gv, 4:5], ALU.mult, ALU.add)
                            else:
                                last = nc.vector.scalar_tensor_tensor(dst, src, w, dst, ALU.mult, ALU.add)
                            if tap == 2 and gv == 0:
                                last.then_inc(gate_ready, 1)
                        if tap < 2:
                            link(last)
                    last.then_inc(conv_read, 1)
                    dve.wait_ge(conv_read, 2 + n + 1)
                    dve.wait_ge(gelu_done, n + 1)
                    nc.vector.tensor_tensor(gT[:, ds(f, 1), :].rearrange("p a n -> p (a n)"), cv[:, par, 0, :],
                                            cv[:, par, 1, :], ALU.mult).then_inc(gT_ready, 1)

                over_chunks(dve, b, chunk)
                dve.wait_ge(r_in, 16 * tiles * (b + 1))
                for half in range(2):
                    dve.wait_ge(down_done, 2 + LOADS * b + (half + 1) * (FC // WG))
                    for k in range(tiles):
                        part = r[0:rows, k, half * 512:(half + 1) * 512]
                        nc.vector.scalar_tensor_tensor(part, part, ALPHA, ps[0:rows, k // 2, k % 2, :],
                                                       ALU.mult, ALU.add).then_inc(y_read, 1)
                dve.wait_ge(y_read, 2 * tiles * (b + 1))
                norm_link.enter(norm.STEPS * tiles * b)
                for k in range(tiles):
                    norm.vector(dve, norm_link, r[0:rows, k, :], tiles * b + k, k % 2, rows)

            over_blocks(dve, body)

        @block.gpsimd
        def _(pool):
            if sample:
                pool.wait_ge(s_in, 16)
            else:
                nc.gpsimd.memset(hist[:, :, :, :, :], 0.0).then_inc(hist_ready, 1)
                pool.wait_ge(hist_ready, 1)
            pool.wait_ge(g_in, 32)

            def body(b):
                def chunk(f, n, turn, par):
                    kept = hist[:, ds(f, 1), :, :, :].rearrange("p a g s t -> p (a g) s t")
                    pool.wait_ge(conv_read, n + 1)
                    pool.wait_ge(tails, n + 2)
                    nc.gpsimd.tensor_tensor(spare[:, :], zero[:, :], zero[:, :], ALU.add)
                    nc.gpsimd.tensor_copy(h[:, par, :, :, 0:2], kept).then_inc(halos, 1)
                    pool.wait_ge(halos, n + 1)
                    pool.wait_ge(up_out, 4 + 2 * n + 2)
                    nc.gpsimd.tensor_tensor(spare[:, :], zero[:, :], zero[:, :], ALU.add)
                    nc.gpsimd.tensor_copy(kept, h[:, par, :, :, T:T + 2]).then_inc(tails, 1)

                over_chunks(pool, b, chunk)
                for k in range(tiles):
                    norm.pool(pool, r[0:rows, k, :], tiles * b + k, rows)

            over_blocks(pool, body)


def constants():
    r = np.arange(P)
    c = {}
    f = np.float32
    c["c_ident"] = np.eye(P, dtype=f)
    c["c_upto"] = (r[:, None] <= r[None, :]).astype(f)
    c["c_before"] = ((r[:, None] % H == r[None, :] % H) & (r[:, None] // H < r[None, :] // H)).astype(f)
    q = np.arange(S)
    c["c_uptos"] = ((q[:, None] // NT == q[None, :] // NT) & (q[:, None] <= q[None, :])).astype(f)
    t = np.arange(MAXW)
    wins = 2 ** (np.arange(G) + 1)
    c["c_cnt"] = np.broadcast_to(wins[:, None] / np.minimum(t[None, :] + 1, wins[:, None]), (P, G, MAXW)).astype(f).copy()
    c["c_later"] = (r[:, None] > r[None, :]).astype(f)
    c["c_latep"] = ((r[:, None] // NPG == r[None, :] // NPG) & (r[:, None] > r[None, :])).astype(f)
    hs, b, q = r // 32, r // 8 % 4, r % 8
    st_o, hs_o, q_o = r // 64, r // 8 % 4, r % 8
    c["c_sel"] = np.stack([(r[:, None] // 32 == b[None, :]) & (r[:, None] % 32 == 4 * st + hs[None, :])
                           for st in range(2)], 1).astype(f)
    c["c_seln"] = np.stack([r[0:32, None] == 4 * st + hs[None, :] for st in range(2)], 1).astype(f)
    c["c_lsel"] = np.stack([(st_o[None, :] == st) & (hs_o[None, :] == hs[:, None]) & (q_o[None, :] == q[:, None])
                            for st in range(2)], 1).astype(f)
    e = np.arange(16)
    c["c_osel"] = np.stack([(st_o[:, None] == k // 2) & (hs_o[:, None] == 2 * (k % 2) + e[None, :] // 8)
                            & (q_o[:, None] == e[None, :] % 8) for k in range(AC)], 1).astype(f)
    key = np.arange(32)
    c["c_nmask"] = np.where((key[None, :] // 8 == b[:, None]) & (key[None, :] % 8 <= q[:, None]), 0.0, NEG).astype(mybir.dt.np(BF16))
    c["c_rowmask"] = np.where(b[:, None] == np.arange(NB)[None, :] % 4, 0.0, NEG).astype(f)
    c["c_identb"] = np.eye(P).astype(mybir.dt.np(BF16))
    c["c_causal"] = np.where(r[:, None] >= r[None, :], 0.0, NEG).astype(mybir.dt.np(BF16))
    return c


def lay_out_ffn(a):
    f32 = np.ascontiguousarray
    cols = np.stack([a["b_up"][0]] + [a["w_conv"][0, j] for j in range(3)] + [a["b_conv"][0]])
    return {"w_up_t": f32(a["w_up"][0].reshape(DC, P, 2, FC, P).transpose(3, 1, 2, 0, 4)),
            "coef_t": f32(cols.reshape(5, 2, FC, P).transpose(2, 3, 1, 0)),
            "state_conv_t": f32(a["state_conv"][0].reshape(NB, 2, 2, FC, P).transpose(4, 3, 2, 0, 1))}


def build(nc, io, sc):
    with ExitStack() as outer:
        m = Mem(nc, outer, "all")
        persist = {"ident": m.sb("ident", [P, P]), "identb": m.sb("identb", [P, P], BF16),
                   "causal": m.sb("causal", [P, P], BF16), "attT_s": m.sb("attT_s", [P, AC, S]),
                   "snew": m.sb("snew", [P, NB, 2, 32])}
        identb_in = m.sem("identb_in")
        with nc.Block() as block:
            @block.sync
            def _(sp):
                sp.dma_start(persist["identb"][:, :], io["c_identb"]).then_inc(identb_in, 16)
                sp.wait_ge(identb_in, 16)
        with ExitStack() as ctx:
            pm = Mem(nc, ctx, "AB")
            persist["uT"] = pm.sb("uT", [P, G, MAXW + SEQ])
            persist["fgate"] = pm.sb("fgate", [P, TILES + 1, H])
            persist["psamp"] = pm.sb("psamp", [P, IW])
            persist["uTs"] = pm.sb("uTs", [P, G, NB, MAXW - 1 + NT])
            stage_project(nc, io, sc, persist)
            stage_gates_pool(nc, io, sc, persist)
        stage_prepare(nc, io, sc, persist)
        stage_attention(nc, io, sc, persist)
        stage_mix(nc, io, sc, persist, False)
        stage_decode(nc, io, sc, persist)
        stage_mix(nc, io, sc, persist, True)
        stage_ffn(nc, io, sc, persist, False)
        stage_ffn(nc, io, sc, persist, True)


OUTPUTS = {"y_prompt": (SEQ, D), "y_sample": (S, D), "k_prompt": (SEQ, AW), "v_prompt": (SEQ, AW),
           "logf_prompt": (SEQ, H), "pool_prompt": (MAXW - 1, PW), "conv_prompt": (P, FC, 2, 1, 2),
           "k_sample": (S, AW), "v_sample": (S, AW), "logf_sample": (S, H),
           "pool_sample": (NB, MAXW - 1, PW), "conv_sample": (P, FC, 2, NB, 2)}
SCRATCH = {"qkT": (2 * AC, P, SEQ), "q_s": (S, AW), "aug": (H, 4, SEQ), "negc_s": (S, H),
           "poolT": (TILES + 1, P, G, P), "att": (SEQ, AW), "x1": (SEQ + S, D), "x1T": (TILES + 1, P, DC, P),
           "qbd": (NB, P, 16 * 32), "wT": (NB // 2, P, P * 32), "vgrp": (NB, 32, AW)}


def kernel(**inputs):
    import concourse.bacc as bacc
    from concourse.bass_utils import run_bass_kernel_spmd

    a = {name: np.asarray(x) for name, x in inputs.items()}
    arrays = {name: a[name] for name in ("x_prompt", "x_sample", "state_pool", "w_in", "b_f", "w_pool", "w_out",
                                         "ln1_g", "ln1_b", "w_down", "ln2_g", "ln2_b")}
    arrays["pool_scale_t"] = a["pool_scale"][0].reshape(G, P).T
    arrays["cache_k"] = a["cache_k"][0].reshape(NPOOL, PAGE, AW)
    arrays["cache_v"] = a["cache_v"][0].reshape(NPOOL, PAGE, AW)
    arrays["cache_logf"] = a["cache_logf"][0].reshape(NPOOL, PAGE * H)
    arrays["page_ids"] = a["page_table"].reshape(1, NB * NPG)
    arrays["page_rows"] = a["page_table"].reshape(NB // 2, P).T
    arrays.update(lay_out_ffn(a))
    arrays.update(constants())
    arrays = {name: np.ascontiguousarray(x) for name, x in arrays.items()}

    nc = bacc.Bacc("TRN2", target_bir_lowering=False, num_devices=1)
    io = {name: nc.dram_tensor(name, x.shape, mybir.dt.from_np(x.dtype), kind="ExternalInput").ap()
          for name, x in arrays.items()}
    io.update({name: nc.dram_tensor(name, shape, F32, kind="ExternalOutput").ap() for name, shape in OUTPUTS.items()})
    sc = {name: nc.dram_tensor("sc_" + name, shape, F32, kind="Internal").ap() for name, shape in SCRATCH.items()}
    build(nc, io, sc)
    r = run_bass_kernel_spmd(nc, [arrays], core_ids=[0]).results[0]
    heads = (H, HD)
    return (r["y_prompt"].reshape(1, SEQ, D), r["y_sample"].reshape(NB, NT, D),
            r["k_prompt"].reshape(1, 1, SEQ, *heads), r["v_prompt"].reshape(1, 1, SEQ, *heads),
            r["logf_prompt"].reshape(1, 1, SEQ, H), r["pool_prompt"].reshape(1, 1, MAXW - 1, PW),
            r["conv_prompt"].transpose(3, 4, 2, 1, 0).reshape(1, 1, 2, 2 * FF),
            r["k_sample"].reshape(1, NB, NT, *heads), r["v_sample"].reshape(1, NB, NT, *heads),
            r["logf_sample"].reshape(1, NB, NT, H), r["pool_sample"].reshape(1, NB, MAXW - 1, PW),
            r["conv_sample"].transpose(3, 4, 2, 1, 0).reshape(1, NB, 2, 2 * FF))
```
